# Optimizing a Trainium2 kernel written in Bass

```python
import jax, jax.numpy as jnp
from jax import lax
import numpy as np

D_MODEL = 1024
BATCH = 1
SEQ = 256
DEPTH = 1
DEC_BATCH = 8
DEC_SEQ = 8
PAST_LEN = 2048
PAGE_SIZE = 128

SSD_EXPAND = 2
D_INNER = SSD_EXPAND * D_MODEL
SSD_HEAD_DIM = 64
SSD_HEADS = D_INNER // SSD_HEAD_DIM
SSD_GROUPS = 4
HEADS_PER_GROUP = SSD_HEADS // SSD_GROUPS
D_STATE = 128
CONV_W = 4
CONV_DIM = D_INNER + 2 * SSD_GROUPS * D_STATE
SSD_CHUNK = 128
D_GMLP = D_MODEL
GMLP_HEADS = 8
GMLP_HEAD_DIM = D_GMLP // GMLP_HEADS
GMLP_CHUNK = 128
N_BRANCHES = 2
N_EXPERTS = 32
TOP_K = 4
D_FF = D_MODEL
SWIGLU_ALPHA = 1.702
SWIGLU_LIMIT = 7.0
MOE_BLOCK = 128
EPS = 1e-5
SPLIT_Z = D_INNER
SPLIT_XBC = SPLIT_Z + CONV_DIM
SPLIT_DT = SPLIT_XBC + SSD_HEADS
SPLIT_UV = SPLIT_DT + 2 * D_GMLP
D_IN_PROJ = SPLIT_UV + N_BRANCHES * D_MODEL

kernel_name = "hybrid_ssd_gmlp_moe_step"

def rmsnorm(x, w):
    xf = x.astype(jnp.float32)
    y = xf * lax.rsqrt(jnp.mean(xf * xf, axis=-1, keepdims=True) + EPS)
    return (y * w.astype(jnp.float32)).astype(x.dtype)

def layernorm(x, w, b):
    xf = x.astype(jnp.float32)
    mu = jnp.mean(xf, axis=-1, keepdims=True)
    xc = xf - mu
    y = xc * lax.rsqrt(jnp.mean(xc * xc, axis=-1, keepdims=True) + EPS)
    return (y * w.astype(jnp.float32) + b.astype(jnp.float32)).astype(x.dtype)

def ssd_chunked(x, dt, a_log, b_in, c_in, init_state):
    f32 = jnp.float32
    bsz, l = x.shape[0], x.shape[1]
    q = SSD_CHUNK if l % SSD_CHUNK == 0 else l
    nc = l // q
    G, R, P, N = SSD_GROUPS, HEADS_PER_GROUP, SSD_HEAD_DIM, D_STATE
    a = dt * (-jnp.exp(a_log.astype(f32)))
    a_cum = jnp.cumsum(a.reshape(bsz, nc, q, SSD_HEADS), axis=2)
    xdt = (x.astype(f32) * dt[..., None]).reshape(bsz, nc, q, G, R, P)
    bc = b_in.astype(f32).reshape(bsz, nc, q, G, N)
    cc = c_in.astype(f32).reshape(bsz, nc, q, G, N)
    causal = jnp.tril(jnp.ones((q, q), bool))[None, None, :, :, None]
    seg = a_cum[:, :, :, None, :] - a_cum[:, :, None, :, :]
    decay = jnp.exp(jnp.where(causal, seg, -jnp.inf)).reshape(bsz, nc, q, q, G, R)
    cb = jnp.einsum('bclgn,bcsgn->bclsg', cc, bc)
    y_diag = jnp.einsum('bclsgr,bcsgrp->bclgrp', cb[..., None] * decay, xdt)
    decay_end = jnp.exp(a_cum[:, :, -1:, :] - a_cum).reshape(bsz, nc, q, G, R)
    chunk_states = jnp.einsum('bclgn,bclgrp->bcgrpn', bc, xdt * decay_end[..., None])
    chunk_decay = jnp.exp(a_cum[:, :, -1, :]).reshape(bsz, nc, G, R)

    def carry_step(s, inp):
        st, dec = inp
        return s * dec[..., None, None] + st, s

    s0 = init_state.astype(f32).reshape(bsz, G, R, P, N)
    s_final, s_start = lax.scan(carry_step, s0,
                                (jnp.moveaxis(chunk_states, 1, 0), jnp.moveaxis(chunk_decay, 1, 0)))
    s_start = jnp.moveaxis(s_start, 0, 1)
    y_off = jnp.einsum('bclgn,bcgrpn->bclgrp', cc, s_start) * jnp.exp(a_cum).reshape(bsz, nc, q, G, R)[..., None]
    y = (y_diag + y_off).reshape(bsz, l, SSD_HEADS, P)
    return y, s_final.reshape(bsz, SSD_HEADS, P, N)

def chunk_gmlp(u, v, w_spatial, b_spatial):
    bsz, l, _ = v.shape
    lp = -(-l // GMLP_CHUNK) * GMLP_CHUNK
    vp = jnp.pad(v, ((0, 0), (0, lp - l), (0, 0))).reshape(bsz, lp // GMLP_CHUNK, GMLP_CHUNK, GMLP_HEADS, GMLP_HEAD_DIM)
    ws = jnp.where(jnp.tril(jnp.ones((GMLP_CHUNK, GMLP_CHUNK), bool))[None], w_spatial, 0).astype(v.dtype)
    mixed = jnp.einsum('gts,bcsgd->bctgd', ws, vp) + b_spatial.T.astype(v.dtype)[None, None, :, :, None]
    mixed = mixed.reshape(bsz, lp, D_GMLP)[:, :l]
    return u * mixed

def moe_ffn(h, w_router, b_router, w_gu, b_gu, w_down, b_down):
    f32 = jnp.float32
    t = h.shape[0]
    logits = jnp.dot(h.astype(f32), w_router.astype(f32)) + b_router.astype(f32)
    top_logit, top_e = lax.top_k(logits, TOP_K)
    gate = jax.nn.softmax(top_logit, axis=-1)
    n_assign = t * TOP_K
    flat_e = top_e.reshape(-1)
    order = jnp.argsort(flat_e)
    sorted_e = flat_e[order]
    counts = jnp.bincount(flat_e, length=N_EXPERTS)
    padded = (counts + MOE_BLOCK - 1) // MOE_BLOCK * MOE_BLOCK
    padded_end = jnp.cumsum(padded)
    padded_start = padded_end - padded
    start = jnp.cumsum(counts) - counts
    slot = padded_start[sorted_e] + jnp.arange(n_assign) - start[sorted_e]
    n_blocks = -(-n_assign // MOE_BLOCK) + N_EXPERTS
    n_slots = n_blocks * MOE_BLOCK
    slot_tok = jnp.zeros((n_slots,), jnp.int32).at[slot].set((order // TOP_K).astype(jnp.int32))
    slot_gate = jnp.zeros((n_slots,), f32).at[slot].set(gate.reshape(-1)[order])
    block_e = jnp.minimum(jnp.searchsorted(padded_end, jnp.arange(n_blocks) * MOE_BLOCK, side='right'), N_EXPERTS - 1)
    xs = h[slot_tok].reshape(n_blocks, MOE_BLOCK, D_MODEL)

    def expert_block(args):
        xb, e = args
        gu = xb @ w_gu[e] + b_gu[e]
        glu = jnp.minimum(gu[:, 0::2], SWIGLU_LIMIT)
        lin = jnp.clip(gu[:, 1::2], -SWIGLU_LIMIT, SWIGLU_LIMIT)
        act = glu * jax.nn.sigmoid(SWIGLU_ALPHA * glu) * (lin + 1)
        return act @ w_down[e] + b_down[e]

    ys = lax.map(expert_block, (xs, block_e)).reshape(n_slots, D_MODEL)
    ys = (ys.astype(f32) * slot_gate[:, None]).astype(h.dtype)
    return jnp.zeros_like(h).at[slot_tok].add(ys)

def hybrid_layer(x, conv_prefix, ssm_init, norm_mix, w_in, conv_w, conv_b, dt_bias, a_log, d_skip, gnorm_w,
                 v_norm_w, v_norm_b, w_spatial, b_spatial, w_branch_ssd, w_branch_mlp, w_out,
                 norm_ffn, w_router, b_router, w_gu, b_gu, w_down, b_down):
    bsz, l, _ = x.shape
    hn = rmsnorm(x, norm_mix)
    proj = hn @ w_in
    z, xbc, dt_raw, uv, gates = jnp.split(proj, [SPLIT_Z, SPLIT_XBC, SPLIT_DT, SPLIT_UV], axis=-1)
    xpad = jnp.concatenate([conv_prefix.astype(xbc.dtype), xbc], axis=1)
    new_conv = xpad[:, -(CONV_W - 1):]
    conv = conv_b
    for k in range(CONV_W):
        conv = conv + xpad[:, k:k + l] * conv_w[k]
    xbc_act = jax.nn.silu(conv)
    xs, b_ssm, c_ssm = jnp.split(xbc_act, [D_INNER, D_INNER + SSD_GROUPS * D_STATE], axis=-1)
    xs = xs.reshape(bsz, l, SSD_HEADS, SSD_HEAD_DIM)
    dt = jax.nn.softplus(dt_raw.astype(jnp.float32) + dt_bias.astype(jnp.float32))
    y_ssd, new_ssm = ssd_chunked(xs, dt, a_log, b_ssm.reshape(bsz, l, SSD_GROUPS, D_STATE),
                                 c_ssm.reshape(bsz, l, SSD_GROUPS, D_STATE), ssm_init)
    y_ssd = y_ssd + d_skip.astype(jnp.float32)[:, None] * xs.astype(jnp.float32)
    y_ssd = y_ssd.reshape(bsz, l, D_INNER).astype(x.dtype)
    y_ssd = rmsnorm(y_ssd * jax.nn.silu(z), gnorm_w)
    uv = jax.nn.gelu(uv, approximate=False)
    u, v = jnp.split(uv, 2, axis=-1)
    v = layernorm(v, v_norm_w, v_norm_b)
    y_mlp = chunk_gmlp(u, v, w_spatial, b_spatial)
    g_ssd, g_mlp = jnp.split(jax.nn.sigmoid(gates), 2, axis=-1)
    merged = g_ssd * (y_ssd @ w_branch_ssd) + g_mlp * (y_mlp @ w_branch_mlp)
    h = x + merged @ w_out
    hf = rmsnorm(h, norm_ffn).reshape(bsz * l, D_MODEL)
    h = h + moe_ffn(hf, w_router, b_router, w_gu, b_gu, w_down, b_down).reshape(bsz, l, D_MODEL)
    return h, new_conv, new_ssm.astype(ssm_init.dtype), v

def setup_inputs(seed: int = 0) -> dict:
    key = jax.random.key(seed)
    ks = jax.random.split(key, 32)
    f32 = jnp.float32
    nrm = lambda k, shape, s: jax.random.normal(k, shape, f32) * s
    dt0 = jnp.exp(jax.random.uniform(ks[7], (DEPTH, SSD_HEADS), f32, np.log(1e-3), np.log(1e-1)))
    return {
        "x_prompt": nrm(ks[0], (BATCH, SEQ, D_MODEL), 1.0),
        "x_sample": nrm(ks[1], (DEC_BATCH, DEC_SEQ, D_MODEL), 1.0),
        "state_conv": nrm(ks[2], (DEPTH, DEC_BATCH, CONV_W - 1, CONV_DIM), 1.0),
        "state_ssm": nrm(ks[3], (DEPTH, DEC_BATCH, SSD_HEADS, SSD_HEAD_DIM, D_STATE), 0.5),
        "norm_mix": 1.0 + nrm(ks[4], (DEPTH, D_MODEL), 0.05),
        "w_in": nrm(ks[5], (DEPTH, D_MODEL, D_IN_PROJ), D_MODEL ** -0.5),
        "conv_w": nrm(ks[6], (DEPTH, CONV_W, CONV_DIM), CONV_W ** -0.5),
        "conv_b": nrm(ks[8], (DEPTH, CONV_DIM), 0.02),
        "dt_bias": dt0 + jnp.log(-jnp.expm1(-dt0)),
        "a_log": jnp.log(jax.random.uniform(ks[9], (DEPTH, SSD_HEADS), f32, 1.0, 16.0)),
        "d_skip": 1.0 + nrm(ks[10], (DEPTH, SSD_HEADS), 0.05),
        "gnorm_w": 1.0 + nrm(ks[11], (DEPTH, D_INNER), 0.05),
        "v_norm_w": 1.0 + nrm(ks[12], (DEPTH, D_GMLP), 0.05),
        "v_norm_b": nrm(ks[13], (DEPTH, D_GMLP), 0.02),
        "w_spatial": nrm(ks[14], (DEPTH, GMLP_HEADS, GMLP_CHUNK, GMLP_CHUNK), GMLP_CHUNK ** -0.5),
        "b_spatial": 1.0 + nrm(ks[15], (DEPTH, GMLP_HEADS, GMLP_CHUNK), 0.1),
        "w_branch_ssd": nrm(ks[16], (DEPTH, D_INNER, D_MODEL), D_INNER ** -0.5),
        "w_branch_mlp": nrm(ks[17], (DEPTH, D_GMLP, D_MODEL), D_GMLP ** -0.5),
        "w_out": nrm(ks[18], (DEPTH, D_MODEL, D_MODEL), D_MODEL ** -0.5),
        "norm_ffn": 1.0 + nrm(ks[19], (DEPTH, D_MODEL), 0.05),
        "w_router": nrm(ks[20], (DEPTH, D_MODEL, N_EXPERTS), D_MODEL ** -0.5),
        "b_router": nrm(ks[21], (DEPTH, N_EXPERTS), 0.01),
        "w_gu": nrm(ks[22], (DEPTH, N_EXPERTS, D_MODEL, 2 * D_FF), D_MODEL ** -0.5),
        "b_gu": nrm(ks[23], (DEPTH, N_EXPERTS, 2 * D_FF), 0.01),
        "w_down": nrm(ks[24], (DEPTH, N_EXPERTS, D_FF, D_MODEL), D_FF ** -0.5),
        "b_down": nrm(ks[25], (DEPTH, N_EXPERTS, D_MODEL), 0.01),
        "norm_final": 1.0 + nrm(ks[26], (D_MODEL,), 0.05),
    }

def reference(x_prompt, x_sample, state_conv, state_ssm, norm_mix, w_in, conv_w, conv_b, dt_bias, a_log,
              d_skip, gnorm_w, v_norm_w, v_norm_b, w_spatial, b_spatial, w_branch_ssd, w_branch_mlp, w_out,
              norm_ffn, w_router, b_router, w_gu, b_gu, w_down, b_down, norm_final):
    hp, hs = x_prompt, x_sample
    conv_p, ssm_p, conv_s, ssm_s, v_s = [], [], [], [], []
    for i in range(DEPTH):
        params = (norm_mix[i], w_in[i], conv_w[i], conv_b[i], dt_bias[i], a_log[i], d_skip[i], gnorm_w[i],
                  v_norm_w[i], v_norm_b[i], w_spatial[i], b_spatial[i], w_branch_ssd[i], w_branch_mlp[i],
                  w_out[i], norm_ffn[i], w_router[i], b_router[i], w_gu[i], b_gu[i], w_down[i], b_down[i])
        zero_conv = jnp.zeros((hp.shape[0], CONV_W - 1, CONV_DIM), hp.dtype)
        zero_ssm = jnp.zeros((hp.shape[0], SSD_HEADS, SSD_HEAD_DIM, D_STATE), state_ssm.dtype)
        hp, cp, sp, _ = hybrid_layer(hp, zero_conv, zero_ssm, *params)
        hs, cs, ss, vs = hybrid_layer(hs, state_conv[i], state_ssm[i], *params)
        conv_p.append(cp); ssm_p.append(sp); conv_s.append(cs); ssm_s.append(ss); v_s.append(vs)
    y_prompt = rmsnorm(hp, norm_final)
    y_sample = rmsnorm(hs, norm_final)
    return (y_prompt, y_sample, jnp.stack(conv_p), jnp.stack(ssm_p), jnp.stack(conv_s), jnp.stack(ssm_s), jnp.stack(v_s))


_drawn_inputs = setup_inputs


def setup_inputs(seed=0):
    import zlib

    import numpy as np

    out = dict(_drawn_inputs(seed))
    spreads = {}
    factors = {'v_norm_b': 2.751, 'b_gu': 8.0, 'b_down': 8.0, 'b_router': 2.769}
    for name, (base, spread) in spreads.items():
        noise = np.random.default_rng([zlib.crc32(name.encode()), seed]).standard_normal(out[name].shape)
        drawn = base * np.exp(spread * noise) if base else spread * noise
        out[name] = __import__('jax').numpy.asarray(drawn.astype(out[name].dtype))
    for name, factor in factors.items():
        out[name] = (out[name] * factor).astype(out[name].dtype)
    return out
```

```python
from contextlib import ExitStack

import concourse.bass as bass
from concourse import mybir

ALU = mybir.AluOpType
ACT = mybir.ActivationFunctionType
F32 = mybir.dt.float32
I32 = mybir.dt.int32
BF16 = mybir.dt.bfloat16
AX = mybir.AxisListType

P = 128
D = 1024
KD = D // P
SEQ, DB, DS = 256, 8, 8
NS = DB * DS
T = SEQ + NS
TILES = [(0, P), (P, P), (SEQ, NS)]
DI = 2 * D
H, HP, G, N = 32, 64, 4, 128
PAIRS = DI // P
CONV = DI + 2 * G * N
CT = CONV // P
TAPS = 4
CG = 6
KEEP = TAPS - 1
STATE_ROWS = KEEP * (1 + DB)
SPAN = KEEP + SEQ
STEP = KEEP + DS
GH = 8
E, TOPK, FF = 32, 4, 1024
LIMIT, ALPHA = 7.0, 1.702
EPS = 1e-5
Z0, X0, DT0 = 0, DI, DI + CONV
U0 = DT0 + H
V0 = U0 + D
GS0 = V0 + D
GM0 = GS0 + D
RING = 6
SLOT = 2048
EXPERT_CHUNKS = 12
MAX_EXTRA = T * TOPK // P


def mixer_chunks():
    out = [("v", m) for m in range(4)] + [("u", m) for m in range(4)] + [("dt", 0)]
    for g in range(G):
        out += [("x", 2 * g), ("x", 2 * g + 1), ("bc", g), ("z", 2 * g), ("z", 2 * g + 1)]
    for m in range(4):
        out += [("gs", m), ("bs", 2 * m), ("bs", 2 * m + 1), ("gm", m), ("bm", m)]
    return out + [("out", m) for m in range(4)]


CHUNKS = mixer_chunks()
AT = {c: n for n, c in enumerate(CHUNKS)}
N_MIXER = len(CHUNKS)
N_PROJ = AT[("gs", 0)]
USED_MIXER = N_MIXER - N_PROJ


def tiles_through(n):
    return sum(1 if c[0] == "dt" else 2 for c in CHUNKS[:n + 1])


def slot_of(j):
    return (N_MIXER + j) % RING


def slot_uses(slot, before):
    return sum(1 for n in range(before) if n % RING == slot)


def build(nc, x_prompt, x_sample, state_conv, state_ssm, norm_mix, w_in, conv_w, conv_b, dt_bias, a_log,
          d_skip, gnorm_w, v_norm_w, v_norm_b, w_spatial, b_spatial, w_branch_ssd, w_branch_mlp, w_out,
          norm_ffn, w_router, b_router, w_gu, b_gu, w_down, b_down, norm_final,
          y_prompt, y_sample, conv_prompt_new, ssm_prompt_new, conv_sample_new, ssm_sample_new, v_sample_new):
    ctx = ExitStack()
    with ctx:
        def sb(name, shape, dt=F32):
            return ctx.enter_context(nc.sbuf_tensor(name, shape, dt))

        def sem(name):
            return ctx.enter_context(nc.semaphore(name))

        ring = sb("ring", [P, RING, SLOT])
        hid = sb("hid", [P, 3, D])
        ident = sb("ident", [P, P])
        ones = sb("ones", [P, P])
        before = sb("before", [P, P])
        causal = sb("causal", [P, T])
        samebatch = sb("samebatch", [NS, DB])
        repeat = sb("repeat", [DS, NS])
        running = sb("running", [H, T])
        slots_i = sb("slots_i", [P, 3 * P], I32)
        slots = sb("slots", [P, 3 * P])
        small = sb("small", [P, 64])
        bgu_parts = sb("bgu_parts", [96, 2 * FF], BF16)
        pick_bias = sb("pick_bias", [96, P], BF16)
        row_expert = sb("row_expert", [96, P])
        work = sb("work", [1, 64], I32)
        arena_size = 32900
        tail = arena_size - 1800
        arena = sb("arena", [P, arena_size])
        top = [0]

        def place(at, *shape):
            n = 1
            for s in shape:
                n *= s
            top[0] = at + n
            assert top[0] <= arena_size, (at, shape)
            v = arena[:, at:at + n]
            if len(shape) == 2:
                v = v.rearrange("p (a b) -> p a b", a=shape[0])
            if len(shape) == 3:
                v = v.rearrange("p (a b c) -> p a b c", a=shape[0], b=shape[1])
            return v

        def after(*shape):
            return place(top[0], *shape)

        hnT = place(0, KD, T)
        mlpT = after(KD, T)
        base = top[0]
        hn = place(base, 3, D)
        vtok = after(3, D)
        csin = after(CONV)
        vT = after(2, T)
        vw_row = after(D)
        vb_row = after(D)
        nm_row = after(D)
        ws_in = after(GH, P)
        wsT = after(GH, P)
        wsS = after(GH, NS)
        bs_row = after(GH, P)
        junk = after(D)
        yT = place(base, PAIRS, T)
        csout = after(CONV)
        raw = after(2, SPAN + DB * STEP)
        acc = after(2, T)
        pack = after(CG, STATE_ROWS)
        xsT = [after(4, T) for _ in range(2)]
        bcT = [after(2, T) for _ in range(2)]
        cbm = after(T)
        btok = after(3, P)
        bmask = after(DB, N)
        vec_start = top[0]
        s_in = [after(DB, N) for _ in range(2)]
        s_T = [after(DB, P) for _ in range(2)]
        s_new = after(DB, N)
        s_fin = after(2, N)
        s_0T = after(2, P)
        xdt = after(2, 3 * P)
        xw = after(2, 3 * P)
        xf = after(2, P)
        seg = after(2, T)
        dec = after(2, T)
        esb = after(2, T - P)
        off = after(T - P)
        ysum = after(T)
        print_top = top[0]
        dtmp = place(vec_start + 4 * DB * N, 8, T)
        prefix = place(tail, CT, KEEP * DB)
        acumT = after(T)
        eacT = after(T)
        convv = after(CT * (TAPS + 1))
        gn_col = after(PAIRS)
        ds_col = after(PAIRS)
        tm = after(4, 3 * H)
        assert print_top <= tail, print_top
        mergedT = place(base + PAIRS * T, KD, T)
        gate_s = after(2, T)
        gate_m = after(2, T)
        part_s = after(2, T)
        part_m = after(2, T)
        rstd_row = after(T)
        sqacc = place(tail - T, T)
        sq = place(tail - 2 * T, T)
        assert print_top <= tail - 2 * T, print_top
        hf = place(0, 3, D)
        hfT = after(KD, T)
        nf_row = after(D)
        nl_row = after(D)
        wr = after(KD, E)
        br_row = after(E)
        logits = after(3, E + 4)
        swept = after(3, E + 4)
        expd = after(3, E)
        best = after(3, 8)
        chosen = after(3, E)
        gates = after(3, E)
        slot_no = after(3, E)
        gatesT = after(T)
        bd = after(D)
        bgu = after(2 * FF)
        bgu_rest = after(2 * FF)
        junk2 = after(D)
        take = after(3, P)
        give = after(3, P)
        giveT = after(T)
        xeT = after(KD, P)
        glu = after(4, FF // 4)
        lin = after(4, FF // 4)
        sig = after(4, FF // 4)
        actT = after(FF // P, P)
        ye = after(D)
        flags = after(2, E)
        ranks = after(2 * E)
        match = after(MAX_EXTRA, 2 * E)
        codes = after(16)

        bank = [ctx.enter_context(nc.psum_tensor(f"bank{i}", [P, 512], F32)) for i in range(8)]

        slot_full = [sem(f"slot_full{i}") for i in range(RING)]
        chunk_used = sem("chunk_used")
        x_in = sem("x_in")
        rows_in = sem("rows_in")
        vecs_in = sem("vecs_in")
        csin_in = sem("csin_in")
        ws_in_s = sem("ws_in_s")
        heads_in = sem("heads_in")
        moe_in = sem("moe_in")
        consts = sem("consts")
        pool_chain = sem("pool_chain")
        act_chain = sem("act_chain")
        dve_chain = sem("dve_chain")
        dve_loop = sem("dve_loop")
        stored = sem("stored")

        block = ctx.enter_context(nc.Block())
        names = ("x_ss", "x_var", "x_std", "hn_ready", "hnT_psum", "hnT_ready", "vec_psum", "vec_ready",
                 "pre_psum", "pre_ready", "proj_ready", "proj_read", "vT_ready", "vt_psum", "vt_ready",
                 "ln_var", "ln_std", "v_ready", "ws_psum", "ws_ready", "mix_psum", "mix_read",
                 "dt_exp", "dt_abs", "dt_ln", "dt_u", "dt_ready", "acum_ready", "dt_w", "tm_psum", "tm_ready",
                 "raw_ready", "pre_copied", "conv_done", "packed", "conv_act", "z_ready", "cs_psum", "cs_ready",
                 "cb_psum", "cb_ready", "bt_psum", "bt_ready", "bm_ready", "xt_psum", "xw_ready",
                 "head_psum", "seg_ready", "exp_ready", "decay_ready", "e_psum", "e_ready",
                 "sT_psum", "sT_ready", "s0_psum", "s0_ready", "sf_psum", "sf_ready", "sn_psum", "sn_ready",
                 "off_psum", "off_read", "yd_psum", "y_ready", "sq_ready", "sq_psum", "rs_var", "rs_std",
                 "rs_ready", "gates_ready", "merged", "h_ready", "h_ss", "h_var", "h_std",
                 "hf_ready", "hfT_psum", "hfT_ready", "lg_psum", "lg_ready", "ge_ready", "route_ready",
                 "cnt_psum", "rank_psum", "slot_ready", "work_ready", "bd_psum", "bd_done", "gT_psum", "gT_ready",
                 "sel_ready", "xe_psum", "xe_ready", "gu_psum", "glu_ready", "sig_ready", "act_ready", "at_psum",
                 "at_ready", "gv_psum", "gv_ready", "ye_ready", "cm_psum", "cm_done",
                 "y_ss", "y_var", "y_std", "y_out",
                 "bias_ready", "give_ready", "lin_ready", "prod_ready", "all_added")
        S = {n: sem(n) for n in names}
        s_in_full = [sem("s_in_full0"), sem("s_in_full1")]
        s_fin_out = [sem("s_fin_out0"), sem("s_fin_out1")]
        s_new_out = sem("s_new_out")
        v_out = sem("v_out")
        cs_out = sem("cs_out")
        take_chain = sem("take_chain")
        work_chain = sem("work_chain")

        def chain(eng, s):
            n = [0]

            def link(ins):
                n[0] += 1
                ins.then_inc(s, 1)
                eng.wait_ge(s, n[0])
            return link

        w_in_t = w_in[0].rearrange("(k p) n -> p k n", p=P)
        bs_t = w_branch_ssd[0].rearrange("(q k p) n -> q p k n", p=P, k=KD)
        bm_t = w_branch_mlp[0].rearrange("(k p) n -> p k n", p=P)
        out_t = w_out[0].rearrange("(m k p) n -> m p k n", p=P, k=2)
        gu_t = w_gu[0].rearrange("e (j p) n -> p e j n", p=P)
        down_t = w_down[0].rearrange("e (j k p) n -> j p e k n", p=P, k=2)

        def wide(n):
            return ring[:, n % RING, :].rearrange("p (k n) -> p k n", k=KD)

        def pair_rows(s):
            return ring[:, s, :].rearrange("p (k n) -> p k n", k=2)

        def parts_of(kind, m):
            n = AT[(kind, m)]
            if kind in ("u", "v", "x", "z", "gs", "gm"):
                c = {"u": U0, "v": V0, "x": X0, "z": Z0, "gs": GS0, "gm": GM0}[kind] + 256 * m
                return [(wide(n), w_in_t[:, :, c:c + 256])]
            if kind == "dt":
                return [(ring[:, n % RING, 0:KD * H].rearrange("p (k n) -> p k n", k=KD),
                         w_in_t[:, :, DT0:DT0 + H])]
            if kind == "bc":
                b = X0 + DI + m * N
                return [(wide(n)[:, :, 0:N], w_in_t[:, :, b:b + N]),
                        (wide(n)[:, :, N:2 * N], w_in_t[:, :, b + G * N:b + G * N + N])]
            if kind == "bs":
                return [(wide(n), bs_t[m % 2][:, :, 256 * (m // 2):256 * (m // 2) + 256])]
            if kind == "bm":
                return [(wide(n), bm_t[:, :, 256 * m:256 * m + 256])]
            return [(pair_rows(n % RING), out_t[m])]

        filled = [0] * RING
        full_at = []
        for c in CHUNKS:
            s = AT[c] % RING
            filled[s] += 16 * len(parts_of(*c))
            full_at.append(filled[s])

        def chunk_ready(pe, c):
            n = AT[c]
            pe.wait_ge(slot_full[n % RING], full_at[n])

        def expert_slot_ready(pe, n, j):
            s = slot_of(j)
            pe.wait_ge(slot_full[s], n * 32 + (filled[s] + 16 * (j // RING + 1)))

        def rows(c):
            return TILES[c][1]

        def tok(c):
            return slice(TILES[c][0], TILES[c][0] + TILES[c][1])

        def hb(c, half):
            return slice(half * 512, half * 512 + 512)

        Q_DT = 16
        xchan = lambda g, t: (4 * g + t) if t < 4 else (PAIRS + g if t == 4 else PAIRS + G + g)
        col_a, col_b = 0, 16

        @block.sync
        def _(sp):
            sp.dma_start(hid[:, 0:2, :], x_prompt[0].rearrange("(c p) d -> p c d", p=P)).then_inc(x_in, 16)
            sp.dma_start(hid[0:NS, 2, :], x_sample.rearrange("b l d -> (b l) d")).then_inc(x_in, 16)
            for n, c in enumerate(CHUNKS):
                if n >= RING:
                    if n - RING < N_PROJ:
                        sp.wait_ge(S["proj_ready"], tiles_through(n - RING))
                    else:
                        sp.wait_ge(chunk_used, n - RING - N_PROJ + 1)
                for dst, src in parts_of(*c):
                    sp.dma_start(dst, src).then_inc(slot_full[n % RING], 16)

            def load_expert(n, e):
                for j in range(EXPERT_CHUNKS):
                    s = slot_of(j)
                    sp.wait_ge(chunk_used, n * EXPERT_CHUNKS + (USED_MIXER + j - RING + 1))
                    if j < 8:
                        sp.dma_start(ring[:, s, :], gu_t[:, bass.ds(e, 1), j, :].rearrange("p e n -> p (e n)")
                                     ).then_inc(slot_full[s], 16)
                    else:
                        sp.dma_start(pair_rows(s), down_t[j - 8][:, bass.ds(e, 1), :, :].rearrange(
                            "p e k n -> p (e k) n")).then_inc(slot_full[s], 16)

            with sp.Fori(0, E) as e:
                load_expert(e, e)
            sp.wait_ge(S["work_ready"], 1)
            more = sp.value_load(work[0:1, 32:33], min_val=0, max_val=MAX_EXTRA)
            with sp.If(more > 0):
                with sp.Fori(0, more) as i:
                    e = sp.value_load(work[0:1, bass.ds(i, 1)], min_val=0, max_val=E - 1)
                    load_expert(i + E, e)

        @block.gpsimd
        def _(pool):
            link = chain(pool, pool_chain)
            pool.dma_start(nm_row, norm_mix[0].partition_broadcast(P)).then_inc(rows_in, 16)
            pool.dma_start(junk[0:96, 0:P], conv_w[0].rearrange("k (t p) -> (k t) p", p=P)).then_inc(vecs_in, 16)
            pool.dma_start(junk[96:120, 0:P], conv_b[0].rearrange("(t p) -> t p", p=P)).then_inc(vecs_in, 16)
            pool.dma_start(junk[0:PAIRS, P:2 * P], gnorm_w[0].rearrange("(t p) -> t p", p=P)).then_inc(vecs_in, 16)
            pool.dma_start(csin[0:KEEP * DB, :], state_conv[0].rearrange("b k c -> (b k) c")).then_inc(csin_in, 16)
            pool.dma_start(ws_in, w_spatial[0].rearrange("g t s -> t g s")).then_inc(ws_in_s, 16)
            pool.dma_start(bs_row[0:1], b_spatial[0:1]).then_inc(ws_in_s, 16)
            pool.dma_start(vw_row, v_norm_w[0].partition_broadcast(P)).then_inc(heads_in, 16)
            pool.dma_start(vb_row, v_norm_b[0].partition_broadcast(P)).then_inc(heads_in, 16)
            pool.dma_start(small[0:H, 0:1], dt_bias[0].unsqueeze(1)).then_inc(heads_in, 16)
            pool.dma_start(small[0:H, 1:2], a_log[0].unsqueeze(1)).then_inc(heads_in, 16)
            for half in range(2):
                pool.dma_start(ds_col[HP * half:HP * half + HP, :],
                               d_skip[0].rearrange("(j two) -> two j", two=2)[half].partition_broadcast(HP),
                               allow_slow_non_contiguous=True
                               ).then_inc(heads_in, 16)
            link(pool.memset(ident[:], 0.0))
            link(pool.affine_select(out=ident[:], in_=ident[:], compare_op=ALU.not_equal, fill=1.0, base=0,
                                    pattern=[[-1, P]], channel_multiplier=1))
            link(pool.tensor_copy(repeat[:].rearrange("p (b l) -> p b l", b=DB),
                                  ident[0:DS, 0:DS].unsqueeze(1).to_broadcast([DS, DB, DS])))
            link(pool.memset(ones[:], 1.0))
            link(pool.affine_select(out=before[:], in_=ones[:], compare_op=ALU.is_ge, fill=0.0, base=-1,
                                    pattern=[[1, P]], channel_multiplier=-1))
            link(pool.memset(causal[:], 1.0))
            for c in range(2):
                link(pool.affine_select(out=causal[:, tok(c)], in_=causal[:, tok(c)], compare_op=ALU.is_ge,
                                        fill=0.0, base=0, pattern=[[1, P]], channel_multiplier=-1))
            link(pool.affine_select(out=causal[0:NS, SEQ:T], in_=causal[0:NS, SEQ:T], compare_op=ALU.is_ge,
                                    fill=0.0, base=0, pattern=[[1, NS]], channel_multiplier=-1))
            link(pool.affine_select(out=causal[0:NS, SEQ:T], in_=causal[0:NS, SEQ:T], compare_op=ALU.is_ge,
                                    fill=0.0, base=0, pattern=[[-DS, DB], [0, DS]], channel_multiplier=1))
            link(pool.memset(samebatch[:], 1.0))
            link(pool.affine_select(out=samebatch[:], in_=samebatch[:], compare_op=ALU.is_ge, fill=0.0, base=0,
                                    pattern=[[-DS, DB]], channel_multiplier=1))
            link(pool.affine_select(out=samebatch[:], in_=samebatch[:], compare_op=ALU.is_ge, fill=0.0,
                                    base=DS - 1, pattern=[[DS, DB]], channel_multiplier=-1))
            link(pool.memset(running[:], 1.0))
            link(pool.memset(running[:, 0:SEQ:P], 0.0))
            link(pool.memset(running[:, SEQ:T:DS], 0.0))
            link(pool.iota(slots_i[:], pattern=[[1, 3 * P]], base=0, channel_multiplier=0))
            link(pool.tensor_copy(slots[:], slots_i[:]))
            for part in range(3):
                link(pool.iota(slots_i[32 * part:32 * part + 32, 0:P], pattern=[[0, P]], base=0,
                               channel_multiplier=1))
            pool.tensor_copy(row_expert[:], slots_i[0:96, 0:P]).then_inc(consts, 1)

            pool.wait_ge(S["mix_read"], GH)
            link(pool.memset(cbm, 0.0))
            for r in range(2):
                link(pool.memset(raw[:, r, 0:KEEP], 0.0))
            pool.wait_ge(S["pre_ready"], 2)

            def load_state(j):
                if j >= 2:
                    pool.wait_ge(S["sn_ready"], j - 1)
                pool.dma_start(s_in[j % 2], state_ssm[0].rearrange("b h p n -> (h p) b n")[P * j:P * j + P]
                               ).then_inc(s_in_full[j % 2], 16)

            def conv_group(g):
                for t in range(CG):
                    n = g * CG + t
                    r = raw[:, n % 2, SPAN:].rearrange("p (b k) -> p b k", k=STEP)
                    ch = xchan(g, t)
                    if n >= 2:
                        pool.wait_ge(S["conv_done"], n - 1)
                    pool.tensor_copy(r[:, :, 0:KEEP], prefix[:, ch, :].rearrange("p (b k) -> p b k", k=KEEP)
                                     ).then_inc(S["pre_copied"], 1)
                    if g >= 1 and t == 0:
                        pool.wait_ge(S["cs_psum"], g)
                    pool.wait_ge(S["raw_ready"], n + 1)
                    pool.tensor_copy(pack[:, t, 0:KEEP], raw[:, n % 2, SEQ:SEQ + KEEP])
                    pool.tensor_copy(pack[:, t, KEEP:].rearrange("p (b k) -> p b k", k=KEEP),
                                     r[:, :, DS:DS + KEEP]).then_inc(S["packed"], 1)

            def ssd_group(g):
                pool.wait_ge(S["bt_ready"], g + 1)
                if g:
                    pool.wait_ge(S["sn_psum"], 4 * g)
                pool.tensor_tensor(bmask[0:NS], btok[0:NS, 2, :].unsqueeze(1).to_broadcast([NS, DB, N]),
                                   samebatch[:].unsqueeze(2).to_broadcast([NS, DB, N]), ALU.mult
                                   ).then_inc(S["bm_ready"], 1)
                for j in range(4 * g, 4 * g + 4):
                    if j + 1 < PAIRS:
                        load_state(j + 1)
                    pool.wait_ge(S["exp_ready"], j + 1)
                    pool.wait_ge(S["cb_ready"], g + 1)
                    pool.tensor_tensor(dec, dec, cbm.unsqueeze(1).to_broadcast([P, 2, T]), ALU.mult
                                       ).then_inc(S["decay_ready"], 1)
                    pool.wait_ge(S["sn_ready"], j + 1)
                    pool.dma_start(ssm_sample_new[0].rearrange("b h p n -> (h p) b n")[P * j:P * j + P],
                                   s_new).then_inc(s_new_out, 16)
                    pool.wait_ge(S["y_ready"], j + 1)
                    if j == 0:
                        link(pool.tensor_tensor(sqacc, yT[:, j, :], yT[:, j, :], ALU.mult))
                    else:
                        link(pool.tensor_tensor(sq, yT[:, j, :], yT[:, j, :], ALU.mult))
                        link(pool.tensor_tensor(sqacc, sqacc, sq, ALU.add))
                    pool.tensor_scalar(yT[:, j, :], yT[:, j, :], gn_col[:, j:j + 1], None, ALU.mult
                                       ).then_inc(S["sq_ready"], 1)

            load_state(0)
            for step in range(G + 1):
                if step < G:
                    conv_group(step)
                if step:
                    ssd_group(step - 1)
            pool.wait_ge(S["cs_ready"], G)
            pool.dma_start(conv_prompt_new[0, 0], csout[0:KEEP, :]).then_inc(cs_out, 16)
            pool.dma_start(conv_sample_new[0].rearrange("b k c -> (b k) c"), csout[KEEP:STATE_ROWS, :]
                           ).then_inc(cs_out, 16)
            pool.wait_ge(chunk_used, USED_MIXER)
            pool.wait_ge(s_new_out, 16 * PAIRS)
            pool.dma_start(nf_row, norm_ffn[0].partition_broadcast(P)).then_inc(moe_in, 16)
            pool.dma_start(wr, w_router[0].rearrange("(k p) e -> p k e", p=P)).then_inc(moe_in, 16)
            pool.dma_start(br_row, b_router[0].partition_broadcast(P)).then_inc(moe_in, 16)
            pool.dma_start(bgu[0:E, :], b_gu[0]).then_inc(moe_in, 16)
            pool.dma_start(bd[0:E, :], b_down[0]).then_inc(moe_in, 16)
            pool.dma_start(nl_row, norm_final.partition_broadcast(P)).then_inc(moe_in, 16)

        @block.tensor
        def _(pe):
            def turn(out, in_):
                return pe.transpose(out, in_, ident[0:in_.shape[0], 0:in_.shape[0]])

            def project(q, c, t, cols=P):
                if t == 0:
                    chunk_ready(pe, c)
                if q >= 2:
                    pe.wait_ge(S["proj_read"], q - 1)
                n = AT[c]
                for k in range(KD):
                    w = (ring[:, n % RING, k * H:k * H + H] if c[0] == "dt"
                         else wide(n)[:, k, t * P:t * P + P])
                    mm = pe.matmul(bank[q % 2][0:cols, 0:T], w, hnT[:, k, :], start=(k == 0), stop=(k == KD - 1))
                mm.then_inc(S["proj_ready"], 1)

            pe.wait_ge(consts, 1)
            pe.wait_ge(S["hn_ready"], 3)
            for k in range(KD):
                if k >= 2:
                    pe.wait_ge(S["hnT_ready"], k - 1)
                for c in range(3):
                    mm = turn(bank[k % 2][:, tok(c)], hn[0:rows(c), c, k * P:k * P + P])
                mm.then_inc(S["hnT_psum"], 1)
            pe.wait_ge(vecs_in, 48)
            turn(bank[2][:, 0:120], junk[0:120, 0:P])
            turn(bank[2][:, 120:120 + PAIRS], junk[0:PAIRS, P:2 * P]).then_inc(S["vec_psum"], 1)
            pe.wait_ge(csin_in, 16)
            for half in range(2):
                for i in range(CT // 2):
                    ch = half * CT // 2 + i
                    mm = turn(bank[3 + half][:, i * 24:i * 24 + 24], csin[0:KEEP * DB, ch * P:ch * P + P])
                mm.then_inc(S["pre_psum"], 1)
            pe.wait_ge(ws_in_s, 32)
            for g in range(GH):
                mm = turn(bank[5 + g // 4][:, (g % 4) * P:(g % 4) * P + P], ws_in[:, g, :])
            mm.then_inc(S["ws_psum"], 1)
            pe.wait_ge(S["ws_ready"], 1)
            pe.matmul(bank[7][0:NS, 0:GH * DS], repeat[:, :],
                      wsT[0:DS, :, 0:DS], start=True, stop=True).then_inc(S["ws_psum"], 1)

            def turn_v(m):
                pe.wait_ge(S["vT_ready"], m + 1)
                if m >= 2:
                    pe.wait_ge(S["vt_ready"], m - 1)
                if m == 0:
                    pe.wait_ge(S["vec_ready"], 1)
                if m == 1:
                    pe.wait_ge(S["pre_ready"], 2)
                for c in range(3):
                    mm = turn(bank[2 + m % 2][0:rows(c), c * P:c * P + P], vT[:, m % 2, tok(c)])
                mm.then_inc(S["vt_psum"], 1)

            pe.wait_ge(S["hnT_ready"], KD)
            for m in range(8):
                project(m, ("v", m // 2), m % 2)
                if m:
                    turn_v(m - 1)
            turn_v(7)
            for m in range(8):
                project(8 + m, ("u", m // 2), m % 2)
            project(Q_DT, ("dt", 0), 0, H)

            pe.wait_ge(S["v_ready"], 3)
            pe.wait_ge(S["ws_ready"], 2)
            for g in range(GH):
                b = bank[4 + g % 2]
                if g >= 2:
                    pe.wait_ge(S["mix_read"], g - 1)
                if g == 0:
                    pe.wait_ge(S["pre_ready"], 2)
                for c in range(3):
                    w = wsT[:, g, :] if c < 2 else wsS[0:NS, g, :]
                    pe.matmul(b[:, tok(c)], vtok[0:rows(c), c, g * P:g * P + P], w, start=True, stop=False)
                    bias = (bs_row[0:1, g, :] if c < 2
                            else bs_row[0:1, g, 0:DS].unsqueeze(1).to_broadcast([1, DB, DS]))
                    mm = pe.matmul(b[:, tok(c)], ones[0:1, :], bias, start=False, stop=True)
                mm.then_inc(S["mix_psum"], 1)

            pe.wait_ge(S["dt_w"], 1)
            for kind, src in enumerate((0, None, 3, 4)):
                for c in range(3 if kind < 3 else 1):
                    v = acumT[0:H, tok(c)] if src is None else dtmp[0:H, src, tok(c)]
                    mm = turn(bank[2][0:rows(c), kind * 96 + c * H:kind * 96 + c * H + H], v)
            mm.then_inc(S["tm_psum"], 1)

            def conv_group(g):
                q = Q_DT + 1 + 10 * g
                if g:
                    pe.wait_ge(S["sn_ready"], 4 * g - 4)
                for t in range(CG):
                    project(q + t, ("x", 2 * g + t // 2) if t < 4 else ("bc", g), t % 2)
                for t in range(4):
                    project(q + CG + t, ("z", 2 * g + t // 2), t % 2)
                pe.wait_ge(S["packed"], CG * (g + 1))
                if g >= 2:
                    pe.wait_ge(S["xw_ready"], 4 * g - 4)
                    pe.wait_ge(S["seg_ready"], 4 * g - 4)
                else:
                    pe.wait_ge(S["tm_ready"], 1)
                    pe.wait_ge(S["mix_read"], GH)
                    if g == 1:
                        pe.wait_ge(S["cs_ready"], 1)
                for t in range(CG):
                    o = bank[2][0:STATE_ROWS, t * P:t * P + P] if t < 4 else \
                        bank[4][0:STATE_ROWS, (t - 4) * P:(t - 4) * P + P]
                    mm = turn(o, pack[:, t, :])
                mm.then_inc(S["cs_psum"], 1)

            def ssd_group(g):
                x, bc = xsT[g % 2], bcT[g % 2]
                pe.wait_ge(S["conv_act"], CG * (g + 1))
                if g:
                    pe.wait_ge(S["y_ready"], 4 * g)
                    pe.wait_ge(S["s0_ready"], 4 * g)
                    pe.wait_ge(S["sf_ready"], 4 * g)
                else:
                    pe.wait_ge(S["ws_ready"], 2)
                for c in range(3):
                    mm = pe.matmul(bank[7][0:rows(c), tok(c)], bc[:, 0, tok(c)], bc[:, 1, tok(c)],
                                   start=True, stop=True)
                mm.then_inc(S["cb_psum"], 1)
                for c in range(3):
                    mm = turn(bank[6][0:rows(c), c * P:c * P + P], bc[:, 0, tok(c)])
                mm.then_inc(S["bt_psum"], 1)
                pe.wait_ge(S["cs_ready"], min(g + 2, G))
                for jj in range(4):
                    j = 4 * g + jj
                    p = j % 2
                    if j:
                        pe.wait_ge(S["xw_ready"], j)
                    for c in range(3):
                        mm = turn(bank[2][0:rows(c), c * P:c * P + P], x[:, jj, tok(c)])
                    mm.then_inc(S["xt_psum"], 1)
                    if j:
                        pe.wait_ge(S["seg_ready"], j)
                    for hh in range(2):
                        h = 2 * j + hh
                        mm = pe.matmul(bank[3 + hh][:, 0:T], ident[0:H, h:h + 1].to_broadcast([H, P]),
                                       acumT[0:H, :], start=True, stop=True)
                    mm.then_inc(S["head_psum"], 1)
                    if j:
                        pe.wait_ge(S["e_ready"], j)
                        pe.wait_ge(S["off_read"], j)
                    for hh in range(2):
                        h = 2 * j + hh
                        mm = pe.matmul(bank[5][HP * hh:HP * hh + HP, 0:T - P],
                                       ident[0:H, h:h + 1].to_broadcast([H, HP]), eacT[0:H, P:T],
                                       start=True, stop=True)
                    mm.then_inc(S["e_psum"], 1)
                    pe.wait_ge(s_in_full[p], 16 * (j // 2 + 1))
                    if j:
                        pe.wait_ge(S["sn_ready"], j)
                    pe.wait_ge(S["proj_read"], Q_DT + 1 + 10 * min(g + 2, G))
                    for b in range(DB):
                        mm = turn(bank[b // 4][:, (b % 4) * P:(b % 4) * P + P], s_in[p][:, b, :])
                    mm.then_inc(S["sT_psum"], 1)
                    pe.wait_ge(S["bt_ready"], g + 1)
                    pe.wait_ge(S["xw_ready"], j + 1)
                    if j:
                        pe.wait_ge(S["s0_ready"], j)
                        pe.wait_ge(S["sf_ready"], j)
                    pe.matmul(bank[6][:, 0:P], btok[:, 0, :], xw[:, p, 0:P], start=True, stop=True)
                    pe.matmul(bank[6][:, P:2 * P], xf[:, p, :], btok[:, 0, :], start=True, stop=False)
                    pe.matmul(bank[6][:, P:2 * P], xw[:, p, P:2 * P], btok[:, 1, :], start=False, stop=True
                              ).then_inc(S["sf_psum"], 1)
                    pe.wait_ge(S["sT_ready"], j + 1)
                    pe.wait_ge(S["bm_ready"], g + 1)
                    for half in range(2):
                        mm = pe.matmul(bank[half][:, :], xw[0:NS, p, 2 * P:3 * P],
                                       bmask[0:NS, 4 * half:4 * half + 4, :], start=True, stop=True)
                    mm.then_inc(S["sn_psum"], 1)
                    pe.wait_ge(S["s0_ready"], j + 1)
                    pe.wait_ge(S["e_ready"], j + 1)
                    pe.matmul(bank[5][:, T - P:T], s_0T[:, p, :], bc[:, 1, P:2 * P], start=True, stop=True)
                    for b in range(DB):
                        mm = pe.matmul(bank[5][:, T + DS * b:T + DS * b + DS], s_T[p][:, b, :],
                                       bc[:, 1, SEQ + DS * b:SEQ + DS * b + DS], start=True, stop=True)
                    mm.then_inc(S["off_psum"], 1)
                    pe.wait_ge(S["decay_ready"], j + 1)
                    pe.wait_ge(S["cb_ready"], g + 1)
                    if j:
                        pe.wait_ge(S["y_ready"], j)
                    for hh in range(2):
                        for c in range(3):
                            mm = pe.matmul(bank[7][HP * hh:HP * hh + HP, tok(c)],
                                           xdt[0:rows(c), p, c * P + HP * hh:c * P + HP * hh + HP],
                                           dec[0:rows(c), hh, tok(c)], start=True, stop=True)
                    mm.then_inc(S["yd_psum"], 1)

            for step in range(G + 1):
                if step < G:
                    conv_group(step)
                if step:
                    ssd_group(step - 1)

            pe.wait_ge(S["sq_ready"], PAIRS)
            pe.matmul(bank[2][:, 0:T], ones[:, :], sqacc, start=True, stop=True).then_inc(S["sq_psum"], 1)
            pe.wait_ge(S["rs_ready"], 1)
            pe.wait_ge(S["sn_ready"], PAIRS)
            for mm2 in range(4):
                if mm2:
                    pe.wait_ge(S["merged"], 2 * mm2)
                for which, c in enumerate((("gs", mm2), ("bs", 2 * mm2), ("bs", 2 * mm2 + 1), ("gm", mm2),
                                           ("bm", mm2))):
                    n = AT[c]
                    chunk_ready(pe, c)
                    b = (0, 1, 1, 2, 3)[which]
                    for m in range(2):
                        for k in range(KD):
                            src = hnT[:, k, :] if c[0] in ("gs", "gm") else (
                                yT[:, KD * (which - 1) + k, :] if c[0] == "bs" else mlpT[:, k, :])
                            mm = pe.matmul(bank[4 * m + b][:, 0:T], wide(n)[:, k, m * P:m * P + P], src,
                                           start=(k == 0 and which != 2), stop=(k == KD - 1 and which != 1))
                    mm.then_inc(chunk_used, 1)
            pe.wait_ge(S["merged"], 8)
            for m in range(4):
                chunk_ready(pe, ("out", m))
                w = pair_rows(AT[("out", m)] % RING)
                for k in range(2):
                    for c in range(3):
                        for half in range(2):
                            mm = pe.matmul(bank[2 * c + half][0:rows(c), :], mergedT[:, 2 * m + k, tok(c)],
                                           w[:, k, hb(c, half)], start=(m == 0 and k == 0),
                                           stop=(m == 3 and k == 1))
                mm.then_inc(chunk_used, 1)

            pe.wait_ge(S["hf_ready"], 3)
            for k in range(KD):
                if k >= 2:
                    pe.wait_ge(S["hfT_ready"], k - 1)
                for c in range(3):
                    mm = turn(bank[6 + k % 2][:, tok(c)], hf[0:rows(c), c, k * P:k * P + P])
                mm.then_inc(S["hfT_psum"], 1)
            pe.wait_ge(S["hfT_ready"], KD)
            for c in range(3):
                for k in range(KD):
                    mm = pe.matmul(bank[0][0:rows(c), c * H:c * H + E], hfT[:, k, tok(c)], wr[:, k, :],
                                   start=(k == 0), stop=(k == KD - 1))
            mm.then_inc(S["lg_psum"], 1)
            pe.wait_ge(S["route_ready"], 3)
            for c in range(3):
                for i in range(c):
                    pe.matmul(bank[1][0:rows(c), c * H:c * H + E], ones[:, 0:rows(c)], chosen[:, i, :],
                              start=(i == 0), stop=False)
                mm = pe.matmul(bank[1][0:rows(c), c * H:c * H + E], before[0:rows(c), 0:rows(c)],
                               chosen[0:rows(c), c, :], start=(c == 0), stop=True)
            mm.then_inc(S["rank_psum"], 1)
            for c in range(3):
                mm = pe.matmul(bank[2][0:1, 0:E], ones[0:rows(c), 0:1], chosen[0:rows(c), c, :],
                               start=(c == 0), stop=(c == 2))
            mm.then_inc(S["cnt_psum"], 1)
            for c in range(3):
                mm = turn(bank[3][0:E, tok(c)], gates[0:rows(c), c, :])
            mm.then_inc(S["gT_psum"], 1)
            pe.wait_ge(S["gT_ready"], 1)
            for n in range(6):
                c, half = n // 2, n % 2
                if n >= 2:
                    pe.wait_ge(S["bd_done"], n - 1)
                pe.matmul(bank[4 + n % 2][0:rows(c), :], gatesT[0:E, tok(c)], bd[0:E, hb(c, half)],
                          start=True, stop=True).then_inc(S["bd_psum"], 1)

            def dispatch(n):
                pe.wait_ge(S["sel_ready"], n + 1)
                pe.wait_ge(S["xe_ready"], n) if not isinstance(n, int) or n else pe.wait_ge(S["hfT_ready"], KD)
                for k in range(KD):
                    for c in range(3):
                        mm = pe.matmul(bank[6 + k // 4][:, (k % 4) * P:(k % 4) * P + P],
                                       hf[0:rows(c), c, k * P:k * P + P], take[0:rows(c), c, :],
                                       start=(c == 0), stop=(c == 2))
                mm.then_inc(S["xe_psum"], 1)

            def gate_up(n):
                pe.wait_ge(S["xe_ready"], n + 1)
                if isinstance(n, int) and n == 0:
                    pe.wait_ge(S["gT_ready"], 1)
                    pe.wait_ge(S["slot_ready"], 1)
                    pe.wait_ge(S["work_ready"], 1)
                else:
                    pe.wait_ge(S["at_ready"], n)
                    pe.wait_ge(S["gv_ready"], n)
                for j in range(8):
                    expert_slot_ready(pe, n, j)
                    for q in range(4):
                        mm = pe.matmul(bank[q][:, :], xeT[:, j, :], ring[:, slot_of(j), 512 * q:512 * q + 512],
                                       start=(j == 0), stop=False)
                    mm.then_inc(chunk_used, 1)
                pe.wait_ge(S["bias_ready"], n + 1)
                for q in range(4):
                    pe.matmul(bank[q][:, :], pick_bias[:, :], bgu_parts[:, 512 * q:512 * q + 512],
                              start=False, stop=True).then_inc(S["gu_psum"], 1)

            def turn_act(n):
                pe.wait_ge(S["act_ready"], n * 4 + 4)
                for f in range(8):
                    q = f // 2
                    mm = turn(bank[f // 4][:, (f % 4) * P:(f % 4) * P + P], lin[:, q, (f % 2) * P:(f % 2) * P + P])
                mm.then_inc(S["at_psum"], 1)

            def combine(n):
                pe.wait_ge(S["ye_ready"], n + 1)
                pe.wait_ge(S["gv_ready"], n + 1)
                for i in range(6):
                    c, half = i // 2, i % 2
                    if i >= 2:
                        pe.wait_ge(S["cm_done"], n * 6 + (i - 1))
                    pe.matmul(bank[4 + i % 2][0:rows(c), :], giveT[:, tok(c)], ye[:, hb(c, half)],
                              start=True, stop=True).then_inc(S["cm_psum"], 1)

            def turn_give(n):
                pe.wait_ge(S["give_ready"], n + 1)
                for c in range(3):
                    mm = turn(bank[2][:, tok(c)], give[0:rows(c), c, :])
                mm.then_inc(S["gv_psum"], 1)

            def down(n):
                pe.wait_ge(S["at_ready"], n + 1)
                if isinstance(n, int) and n == 0:
                    pe.wait_ge(S["bd_done"], 6)
                else:
                    pe.wait_ge(S["cm_done"], n * 6)
                for j in range(4):
                    expert_slot_ready(pe, n, 8 + j)
                    for k in range(2):
                        for half in range(2):
                            mm = pe.matmul(bank[4 + half][:, :], actT[:, 2 * j + k, :],
                                           pair_rows(slot_of(8 + j))[:, k, hb(0, half)],
                                           start=(j == 0 and k == 0), stop=(j == 3 and k == 1))
                    mm.then_inc(chunk_used, 1)

            def block_of(n, first=False, last=False):
                gate_up(n)
                if not last:
                    dispatch(n + 1)
                turn_act(n)
                if not first:
                    combine(n - 1)
                turn_give(n)
                down(n)

            dispatch(0)
            block_of(0, first=True)
            with pe.Fori(1, E - 1) as n:
                block_of(n)
            block_of(E - 1, last=True)
            combine(E - 1)
            more = pe.value_load(work[0:1, 32:33], min_val=0, max_val=MAX_EXTRA)
            with pe.If(more > 0):
                with pe.Fori(0, more) as i:
                    n = i + E
                    dispatch(n)
                    gate_up(n)
                    turn_act(n)
                    turn_give(n)
                    down(n)
                    combine(n)

        @block.scalar
        def _(act):
            link = chain(act, act_chain)

            def fn(out, in_, f, **kw):
                return act.activation(out, in_, f, **kw)

            act.wait_ge(x_in, 32)
            for c in range(3):
                fn(hnT.rearrange("p a b -> p (a b)")[0:rows(c), 0:D], hid[0:rows(c), c, :], ACT.Square,
                   accum_out=small[0:rows(c), 4 + c:5 + c]).then_inc(S["x_ss"], 1)
                act.wait_ge(S["x_ss"], c + 1)
            for c in range(3):
                act.wait_ge(S["x_var"], c + 1)
                act.sqrt(small[0:rows(c), 8 + c:9 + c], small[0:rows(c), 4 + c:5 + c]).then_inc(S["x_std"], 1)
            for k in range(KD):
                act.wait_ge(S["hnT_psum"], k + 1)
                act.copy(hnT[:, k, :], bank[k % 2][:, 0:T]).then_inc(S["hnT_ready"], 1)
            for m in range(8):
                act.wait_ge(S["proj_ready"], m + 1)
                if m >= 2:
                    act.wait_ge(S["vt_psum"], m - 1)
                fn(vT[:, m % 2, :], bank[m % 2][:, 0:T], ACT.Gelu).then_inc(S["proj_read"], 1)
                act.wait_ge(S["proj_read"], m + 1)
                act.sem_inc(S["vT_ready"], 1)
            for m in range(8):
                act.wait_ge(S["proj_ready"], 9 + m)
                fn(mlpT[:, m, :], bank[m % 2][:, 0:T], ACT.Gelu).then_inc(S["proj_read"], 1)
            for c in range(3):
                act.wait_ge(S["ln_var"], c + 1)
                act.sqrt(small[0:rows(c), 44 + c:45 + c], small[0:rows(c), 40 + c:41 + c]).then_inc(S["ln_std"], 1)
            act.wait_ge(S["dt_abs"], 1)
            fn(dtmp[0:H, 3, :], dtmp[0:H, 2, :], ACT.Exp)
            fn(small[0:H, 2:3], small[0:H, 1:2], ACT.Exp).then_inc(S["dt_exp"], 1)
            act.wait_ge(S["dt_u"], 1)
            fn(dtmp[0:H, 5, :], dtmp[0:H, 4, :], ACT.Ln).then_inc(S["dt_ln"], 1)
            act.wait_ge(S["acum_ready"], 1)
            fn(dtmp[0:H, 3, :], dtmp[0:H, 2, :], ACT.Exp)
            fn(small[0:H, 3:4], acumT[0:H, SEQ - 1:SEQ], ACT.Exp)
            fn(eacT[0:H, :], acumT[0:H, :], ACT.Exp).then_inc(S["dt_exp"], 1)
            act.wait_ge(S["v_ready"], 3)
            act.dma_start(v_sample_new[0].rearrange("b l d -> (b l) d"), vtok[0:NS, 2, :]).then_inc(v_out, 16)
            act.wait_ge(S["mix_read"], GH)
            act.wait_ge(v_out, 16)

            def conv_group(g):
                q = Q_DT + 1 + 10 * g
                if g >= 2:
                    act.wait_ge(S["yd_psum"], 4 * g - 4)
                    act.wait_ge(S["y_ready"], 4 * g - 4)

                def silu(t):
                    n = g * CG + t
                    act.wait_ge(S["conv_done"], n + 1)
                    dst = xsT[g % 2][:, t, :] if t < 4 else bcT[g % 2][:, t - 4, :]
                    fn(dst, acc[:, n % 2, :], ACT.Silu).then_inc(S["conv_act"], 1)

                for t in range(CG):
                    n = g * CG + t
                    b = bank[(q + t) % 2]
                    ch = xchan(g, t)
                    act.wait_ge(S["proj_ready"], q + t + 1)
                    if n >= 2:
                        act.wait_ge(S["conv_done"], n - 1)
                        act.wait_ge(S["packed"], n - 1)
                        act.wait_ge(S["conv_act"], n - 1)
                    act.copy(raw[:, n % 2, KEEP:SPAN], b[:, 0:SEQ])
                    act.copy(raw[:, n % 2, SPAN:].rearrange("p (b k) -> p b k", k=STEP)[:, :, KEEP:],
                             b[:, SEQ:T].rearrange("p (b k) -> p b k", k=DS)).then_inc(S["raw_ready"], 1)
                    fn(acc[:, n % 2, :], b[:, 0:T], ACT.Identity, scale=convv[:, 72 + ch:73 + ch],
                       bias=convv[:, 96 + ch:97 + ch]).then_inc(S["proj_read"], 1)
                    if t:
                        silu(t - 1)
                silu(CG - 1)
                for t in range(4):
                    act.wait_ge(S["proj_ready"], q + CG + t + 1)
                    fn(yT[:, 4 * g + t, :], bank[(q + CG + t) % 2][:, 0:T], ACT.Silu).then_inc(S["proj_read"], 1)
                act.wait_ge(S["cs_psum"], g + 1)
                act.copy(csout[0:STATE_ROWS, 512 * g:512 * g + 512], bank[2][0:STATE_ROWS, :])
                act.copy(csout[0:STATE_ROWS, DI + N * g:DI + N * g + N], bank[4][0:STATE_ROWS, 0:P])
                act.copy(csout[0:STATE_ROWS, DI + (G + g) * N:DI + (G + g) * N + N], bank[4][0:STATE_ROWS, P:2 * P]
                         ).then_inc(S["cs_ready"], 1)

            def ssd_group(g):
                act.wait_ge(S["bt_psum"], g + 1)
                if g:
                    act.wait_ge(S["bm_ready"], g)
                act.copy(btok[:, 0:2, :], bank[6][:, 0:2 * P].rearrange("p (c n) -> p c n", c=2))
                act.copy(btok[0:NS, 2, :], bank[6][0:NS, 2 * P:3 * P]).then_inc(S["bt_ready"], 1)
                for j in range(4 * g, 4 * g + 4):
                    p = j % 2
                    act.wait_ge(S["e_psum"], j + 1)
                    if j >= 2:
                        act.wait_ge(S["sn_ready"], j - 1)
                        act.wait_ge(S["off_read"], j - 1)
                    act.copy(esb[:, p, :], bank[5][:, 0:T - P]).then_inc(S["e_ready"], 1)
                    act.wait_ge(S["seg_ready"], j + 1)
                    if j:
                        act.wait_ge(S["yd_psum"], j)
                    fn(dec, seg, ACT.Exp).then_inc(S["exp_ready"], 1)
                    act.wait_ge(S["sT_psum"], j + 1)
                    if j >= 2:
                        act.wait_ge(S["off_psum"], j - 1)
                    for half in range(2):
                        i = act.copy(s_T[p][:, 4 * half:4 * half + 4, :],
                                     bank[half][:, :].rearrange("p (b n) -> p b n", b=4))
                    i.then_inc(S["sT_ready"], 1)
                    act.wait_ge(S["sf_psum"], j + 1)
                    act.copy(s_0T[:, p, :], bank[6][:, 0:P]).then_inc(S["s0_ready"], 1)
                    if j >= 2:
                        act.wait_ge(s_fin_out[p], 16 * (j // 2))
                    act.copy(s_fin[:, p, :], bank[6][:, P:2 * P]).then_inc(S["sf_ready"], 1)
                    act.wait_ge(S["sf_ready"], j + 1)
                    act.dma_start(ssm_prompt_new[0, 0].rearrange("h p n -> (h p) n")[P * j:P * j + P],
                                  s_fin[:, p, :]).then_inc(s_fin_out[p], 16)

            for step in range(G + 1):
                if step < G:
                    conv_group(step)
                if step:
                    ssd_group(step - 1)
            act.wait_ge(S["rs_var"], 1)
            act.sqrt(rstd_row, rstd_row).then_inc(S["rs_std"], 1)
            act.wait_ge(cs_out, 32)
            for m in range(8):
                act.wait_ge(chunk_used, AT[("bm", m // 2)] - N_PROJ + 1)
                if m >= 2:
                    act.wait_ge(S["merged"], m - 1)
                fn(gate_s[:, m % 2, :], bank[4 * (m % 2)][:, 0:T], ACT.Sigmoid)
                fn(gate_m[:, m % 2, :], bank[4 * (m % 2) + 2][:, 0:T], ACT.Sigmoid).then_inc(S["gates_ready"], 1)
            act.wait_ge(chunk_used, USED_MIXER)
            for c in range(3):
                act.wait_ge(S["h_ready"], c + 1)
                fn(junk2[0:rows(c)], hid[0:rows(c), c, :], ACT.Square,
                   accum_out=small[0:rows(c), 16 + c:17 + c]).then_inc(S["h_ss"], 1)
                act.wait_ge(S["h_ss"], c + 1)
            for c in range(3):
                act.wait_ge(S["h_var"], c + 1)
                act.sqrt(small[0:rows(c), 20 + c:21 + c], small[0:rows(c), 16 + c:17 + c]).then_inc(S["h_std"], 1)
            for k in range(KD):
                act.wait_ge(S["hfT_psum"], k + 1)
                act.copy(hfT[:, k, :], bank[6 + k % 2][:, 0:T]).then_inc(S["hfT_ready"], 1)
            for c in range(3):
                act.wait_ge(S["lg_ready"], c + 1)
                fn(expd[0:rows(c), c, :], logits[0:rows(c), c, 0:E], ACT.Exp,
                   bias=small[0:rows(c), 24 + c:25 + c]).then_inc(S["ge_ready"], 1)
            act.wait_ge(S["gT_psum"], 1)
            act.copy(gatesT[0:E, :], bank[3][0:E, 0:T]).then_inc(S["gT_ready"], 1)

            def read_inputs(n):
                act.wait_ge(S["xe_psum"], n + 1)
                for half in range(2):
                    i = act.copy(xeT[:, 4 * half:4 * half + 4, :],
                                 bank[6 + half][:, :].rearrange("p (k t) -> p k t", k=4))
                i.then_inc(S["xe_ready"], 1)

            def sigmoids(n):
                for q in range(4):
                    act.wait_ge(S["glu_ready"], n * 4 + (q + 1))
                    fn(sig[:, q, :], glu[:, q, :], ACT.Sigmoid, scale=ALPHA).then_inc(S["sig_ready"], 1)

            def read_act(n):
                act.wait_ge(S["at_psum"], n + 1)
                for half in range(2):
                    i = act.copy(actT[:, 4 * half:4 * half + 4, :],
                                 bank[half][:, :].rearrange("p (k t) -> p k t", k=4))
                i.then_inc(S["at_ready"], 1)

            def read_give(n):
                act.wait_ge(S["gv_psum"], n + 1)
                act.copy(giveT, bank[2][:, 0:T]).then_inc(S["gv_ready"], 1)

            def read_out(n):
                act.wait_ge(chunk_used, n * EXPERT_CHUNKS + (USED_MIXER + EXPERT_CHUNKS))
                for half in range(2):
                    i = act.copy(ye[:, hb(0, half)], bank[4 + half][:, :])
                i.then_inc(S["ye_ready"], 1)

            def block_of(n, last=False):
                sigmoids(n)
                if not last:
                    read_inputs(n + 1)
                read_act(n)
                read_give(n)
                read_out(n)

            read_inputs(0)
            block_of(0)
            with act.Fori(1, E - 1) as n:
                block_of(n)
            block_of(E - 1, last=True)
            act.wait_ge(S["work_ready"], 1)
            more = act.value_load(work[0:1, 32:33], min_val=0, max_val=MAX_EXTRA)
            with act.If(more > 0):
                with act.Fori(0, more) as i:
                    n = i + E
                    read_inputs(n)
                    sigmoids(n)
                    read_act(n)
                    read_give(n)
                    read_out(n)
            for c in range(3):
                act.wait_ge(S["all_added"], 1)
                fn(junk2[0:rows(c)], hid[0:rows(c), c, :], ACT.Square,
                   accum_out=small[0:rows(c), 28 + c:29 + c]).then_inc(S["y_ss"], 1)
                act.wait_ge(S["y_ss"], c + 1)
            for c in range(3):
                act.wait_ge(S["y_var"], c + 1)
                act.sqrt(small[0:rows(c), 32 + c:33 + c], small[0:rows(c), 28 + c:29 + c]).then_inc(S["y_std"], 1)
            act.wait_ge(S["y_out"], 3)
            act.dma_start(y_prompt[0].rearrange("(c p) d -> p c d", p=P), hid[:, 0:2, :]).then_inc(stored, 16)
            act.dma_start(y_sample.rearrange("b l d -> (b l) d"), hid[0:NS, 2, :]).then_inc(stored, 16)
            act.wait_ge(stored, 32)
            act.wait_ge(s_fin_out[0], 16 * PAIRS // 2)
            act.wait_ge(s_fin_out[1], 16 * PAIRS // 2)
            act.wait_ge(s_new_out, 16 * PAIRS)
            act.wait_ge(cs_out, 32)

        @block.vector
        def _(dve):
            link = chain(dve, dve_chain)

            def var(dst, n, count):
                return dve.tensor_scalar(dst, dst, 1.0 / count, EPS, ALU.mult, ALU.add)

            for c in range(3):
                dve.wait_ge(S["x_ss"], c + 1)
                var(small[0:rows(c), 4 + c:5 + c], c, D).then_inc(S["x_var"], 1)
            dve.wait_ge(rows_in, 16)
            for c in range(3):
                dve.wait_ge(S["x_std"], c + 1)
                link(dve.reciprocal(small[0:rows(c), 12 + c:13 + c], small[0:rows(c), 8 + c:9 + c]))
                dve.scalar_tensor_tensor(hn[0:rows(c), c, :], hid[0:rows(c), c, :], small[0:rows(c), 12 + c:13 + c],
                                         nm_row[0:rows(c)], ALU.mult, ALU.mult).then_inc(S["hn_ready"], 1)
            dve.wait_ge(S["vec_psum"], 1)
            dve.tensor_copy(convv[:], bank[2][:, 0:120])
            dve.tensor_copy(gn_col[:], bank[2][:, 120:120 + PAIRS]).then_inc(S["vec_ready"], 1)
            for half in range(2):
                dve.wait_ge(S["pre_psum"], half + 1)
                dve.tensor_copy(prefix[:, half * 12:half * 12 + 12, :],
                                bank[3 + half][:, 0:288].rearrange("p (a b) -> p a b", a=12)
                                ).then_inc(S["pre_ready"], 1)
            dve.wait_ge(S["ws_psum"], 1)
            dve.wait_ge(consts, 1)
            for half in range(2):
                i = dve.tensor_tensor(wsT[:, 4 * half:4 * half + 4, :],
                                      bank[5 + half][:, :].rearrange("p (g t) -> p g t", g=4),
                                      causal[:, 0:P].unsqueeze(1).to_broadcast([P, 4, P]), ALU.mult)
            i.then_inc(S["ws_ready"], 1)
            dve.wait_ge(S["ws_psum"], 2)
            dve.tensor_tensor(wsS[0:NS].rearrange("p g (b l) -> p g b l", b=DB),
                              bank[7][0:NS, 0:GH * DS].rearrange("p (g l) -> p g l", g=GH).unsqueeze(2)
                              .to_broadcast([NS, GH, DB, DS]),
                              samebatch[:].unsqueeze(1).unsqueeze(3).to_broadcast([NS, GH, DB, DS]), ALU.mult
                              ).then_inc(S["ws_ready"], 1)
            for m in range(8):
                dve.wait_ge(S["vt_psum"], m + 1)
                b = bank[2 + m % 2]
                dve.tensor_copy(vtok[:, 0:2, m * P:m * P + P], b[:, 0:2 * P].rearrange("p (c n) -> p c n", c=2))
                dve.tensor_copy(vtok[0:NS, 2, m * P:m * P + P], b[0:NS, 2 * P:3 * P]).then_inc(S["vt_ready"], 1)
            dve.wait_ge(S["vt_ready"], 8)
            dve.wait_ge(heads_in, 96)
            stats = ring_stats = small[:, 48:60]
            for c in range(3):
                r = rows(c)
                for half in range(2):
                    i = dve.bn_stats(small[0:r, 48 + 6 * half:54 + 6 * half], vtok[0:r, c, hb(c, half)])
                link(i)
                link(dve.bn_aggr(small[0:r, 34 + 2 * c:36 + 2 * c], small[0:r, 48:60]))
                dve.tensor_scalar(small[0:r, 40 + c:41 + c], small[0:r, 35 + 2 * c:36 + 2 * c], EPS, None, ALU.add
                                  ).then_inc(S["ln_var"], 1)
            for c in range(3):
                r = rows(c)
                dve.wait_ge(S["ln_std"], c + 1)
                link(dve.reciprocal(small[0:r, 60 + c:61 + c], small[0:r, 44 + c:45 + c]))
                link(dve.tensor_scalar(vtok[0:r, c, :], vtok[0:r, c, :], small[0:r, 34 + 2 * c:35 + 2 * c],
                                       small[0:r, 60 + c:61 + c], ALU.subtract, ALU.mult))
                link(dve.tensor_tensor(vtok[0:r, c, :], vtok[0:r, c, :], vw_row[0:r], ALU.mult))
                dve.tensor_tensor(vtok[0:r, c, :], vtok[0:r, c, :], vb_row[0:r], ALU.add
                                  ).then_inc(S["v_ready"], 1)
            dve.wait_ge(S["proj_ready"], Q_DT + 1)
            x, m, u, rest = dtmp[0:H, 0, :], dtmp[0:H, 1, :], dtmp[0:H, 4, :], dtmp[0:H, 6, :]
            dve.tensor_scalar(x, bank[Q_DT % 2][0:H, 0:T], small[0:H, 0:1], None, ALU.add
                              ).then_inc(S["proj_read"], 1)
            dve.wait_ge(S["proj_read"], Q_DT + 1)
            dve.scalar_tensor_tensor(dtmp[0:H, 2, :], x, -1.0, x, ALU.mult, ALU.min).then_inc(S["dt_abs"], 1)
            link(dve.tensor_scalar(m, x, 0.0, None, ALU.max))
            dve.wait_ge(S["dt_exp"], 1)
            dve.tensor_scalar(u, dtmp[0:H, 3, :], 1.0, None, ALU.add).then_inc(S["dt_u"], 1)
            dve.wait_ge(S["dt_u"], 1)
            link(dve.tensor_scalar(rest, u, -1.0, None, ALU.add))
            link(dve.tensor_tensor(rest, dtmp[0:H, 3, :], rest, ALU.subtract))
            link(dve.reciprocal(dtmp[0:H, 7, :], u))
            link(dve.tensor_tensor(rest, rest, dtmp[0:H, 7, :], ALU.mult))
            link(dve.tensor_tensor(rest, rest, m, ALU.add))
            dve.wait_ge(S["dt_ln"], 1)
            link(dve.tensor_tensor(x, dtmp[0:H, 5, :], rest, ALU.add))
            link(dve.tensor_scalar(m, x, small[0:H, 2:3], -1.0, ALU.mult, ALU.mult))
            link(dve.tensor_tensor_scan(acumT[0:H, :], running[:], m, 0.0, ALU.mult, ALU.add))
            for c in range(2):
                e = TILES[c][0] + P - 1
                dve.tensor_scalar(dtmp[0:H, 2, tok(c)], acumT[0:H, tok(c)], -1.0, acumT[0:H, e:e + 1],
                                  ALU.mult, ALU.add)
            dve.tensor_tensor(dtmp[0:H, 2, SEQ:T].rearrange("p (b l) -> p b l", b=DB),
                              acumT[0:H, SEQ + DS - 1:T:DS].unsqueeze(2).to_broadcast([H, DB, DS]),
                              acumT[0:H, SEQ:T].rearrange("p (b l) -> p b l", b=DB), ALU.subtract
                              ).then_inc(S["acum_ready"], 1)
            dve.wait_ge(S["dt_exp"], 2)
            link(dve.tensor_tensor(dtmp[0:H, 3, :], dtmp[0:H, 3, :], x, ALU.mult))
            dve.tensor_scalar(dtmp[0:H, 4, 0:P], dtmp[0:H, 3, 0:P], small[0:H, 3:4], None, ALU.mult
                              ).then_inc(S["dt_w"], 1)
            for g in range(GH):
                dve.wait_ge(S["mix_psum"], g + 1)
                dve.wait_ge(S["proj_read"], 16)
                dve.tensor_tensor(mlpT[:, g, :], mlpT[:, g, :], bank[4 + g % 2][:, 0:T], ALU.mult
                                  ).then_inc(S["mix_read"], 1)
            link(dve.memset(tm[:, :, :], 0.0))
            dve.wait_ge(S["tm_psum"], 1)
            dve.tensor_copy(tm[:, 0:3, 0:2 * H],
                            bank[2][:, 0:288].rearrange("p (a b) -> p a b", a=3)[:, :, 0:2 * H])
            dve.tensor_copy(tm[0:NS, 0:3, 2 * H:3 * H],
                            bank[2][0:NS, 0:288].rearrange("p (a b) -> p a b", a=3)[:, :, 2 * H:3 * H])
            link(dve.tensor_copy(tm[:, 3, 0:H], bank[2][:, 288:288 + H]))
            dve.sem_inc(S["tm_ready"], 1)

            def conv_group(g):
                for t in range(CG):
                    n = g * CG + t
                    ch = xchan(g, t)
                    dve.wait_ge(S["raw_ready"], n + 1)
                    dve.wait_ge(S["pre_copied"], n + 1)
                    dve.wait_ge(S["proj_read"], Q_DT + 2 + 10 * g + t)
                    a = acc[:, n % 2, :]
                    r = raw[:, n % 2, SPAN:].rearrange("p (b k) -> p b k", k=STEP)
                    for k in range(TAPS - 1):
                        w = convv[:, CT * k + ch:CT * k + ch + 1]
                        dve.scalar_tensor_tensor(a[:, 0:SEQ], raw[:, n % 2, k:k + SEQ], w, a[:, 0:SEQ],
                                                 ALU.mult, ALU.add)
                        i = dve.scalar_tensor_tensor(a[:, SEQ:T].rearrange("p (b k) -> p b k", k=DS),
                                                     r[:, :, k:k + DS], w,
                                                     a[:, SEQ:T].rearrange("p (b k) -> p b k", k=DS),
                                                     ALU.mult, ALU.add)
                        if k < TAPS - 2:
                            link(i)
                        else:
                            i.then_inc(S["conv_done"], 1)

            def ssd_group(g):
                dve.wait_ge(S["cb_psum"], g + 1)
                if g:
                    dve.wait_ge(S["decay_ready"], 4 * g)
                dve.tensor_tensor(cbm[:, 0:SEQ], bank[7][:, 0:SEQ], causal[:, 0:SEQ], ALU.mult)
                dve.tensor_tensor(cbm[0:NS, SEQ:T], bank[7][0:NS, SEQ:T], causal[0:NS, SEQ:T], ALU.mult
                                  ).then_inc(S["cb_ready"], 1)
                for j in range(4 * g, 4 * g + 4):
                    p = j % 2
                    jj = j - 4 * g

                    def heads(out, kind, c0, c1, r):
                        f = tm[0:r, kind, c0 * H:c1 * H].rearrange("p (c h) -> p c h", h=H)[:, :, 2 * j:2 * j + 2]
                        return dve.tensor_tensor(
                            out[0:r, c0 * P:c1 * P].rearrange("p (c h d) -> p c h d", h=2, d=HP),
                            bank[2][0:r, c0 * P:c1 * P].rearrange("p (c h d) -> p c h d", h=2, d=HP),
                            f.unsqueeze(3).to_broadcast([r, c1 - c0, 2, HP]), ALU.mult)

                    dve.wait_ge(S["xt_psum"], j + 1)
                    if j >= 2:
                        dve.wait_ge(S["yd_psum"], j - 1)
                    heads(xdt[:, p, :], 0, 0, 2, P)
                    heads(xdt[:, p, :], 0, 2, 3, NS)
                    heads(xw[:, p, :], 2, 0, 2, P)
                    heads(xw[:, p, :], 2, 2, 3, NS)
                    heads(xf[:, p, :], 3, 0, 1, P).then_inc(S["xw_ready"], 1)
                    dve.wait_ge(S["head_psum"], j + 1)
                    if j:
                        dve.wait_ge(S["exp_ready"], j)
                    for hh in range(2):
                        for c in range(3):
                            h = c * H + 2 * j + hh
                            i = dve.tensor_scalar(seg[:, hh, tok(c)], bank[3 + hh][:, tok(c)], tm[:, 1, h:h + 1],
                                                  0.0, ALU.subtract, ALU.min)
                    i.then_inc(S["seg_ready"], 1)
                    dve.wait_ge(S["sn_psum"], j + 1)
                    dve.wait_ge(S["e_ready"], j + 1)
                    if j:
                        dve.wait_ge(s_new_out, 16 * j)
                    for b in range(DB):
                        i = dve.scalar_tensor_tensor(
                            s_new[:, b, :], s_in[p][:, b, :], esb[:, p, P + DS * b + DS - 1:P + DS * b + DS],
                            bank[b // 4][:, (b % 4) * P:(b % 4) * P + P], ALU.mult, ALU.add)
                    i.then_inc(S["sn_ready"], 1)
                    dve.wait_ge(S["off_psum"], j + 1)
                    dve.tensor_tensor(off, bank[5][:, T - P:2 * T - 2 * P], esb[:, p, :], ALU.mult
                                      ).then_inc(S["off_read"], 1)
                    dve.wait_ge(S["yd_psum"], j + 1)
                    dve.wait_ge(heads_in, 96)
                    link(dve.scalar_tensor_tensor(ysum, xsT[g % 2][:, jj, :], ds_col[:, j:j + 1],
                                                  bank[7][:, 0:T], ALU.mult, ALU.add))
                    link(dve.tensor_tensor(ysum[:, P:T], ysum[:, P:T], off, ALU.add))
                    dve.wait_ge(S["proj_read"], Q_DT + 1 + 10 * g + 10)
                    dve.tensor_tensor(yT[:, j, :], yT[:, j, :], ysum, ALU.mult).then_inc(S["y_ready"], 1)

            for step in range(G + 1):
                if step < G:
                    conv_group(step)
                if step:
                    ssd_group(step - 1)

            dve.wait_ge(S["sq_psum"], 1)
            dve.tensor_scalar(rstd_row, bank[2][:, 0:T], 1.0 / DI, EPS, ALU.mult, ALU.add
                              ).then_inc(S["rs_var"], 1)
            dve.wait_ge(S["rs_std"], 1)
            dve.reciprocal(rstd_row, rstd_row).then_inc(S["rs_ready"], 1)
            dve.wait_ge(S["rs_ready"], 1)
            dve.wait_ge(cs_out, 32)
            for m in range(8):
                b = 4 * (m % 2)
                dve.wait_ge(S["gates_ready"], m + 1)
                dve.tensor_tensor(part_s[:, m % 2, :], gate_s[:, m % 2, :], bank[b + 1][:, 0:T], ALU.mult)
                link(dve.tensor_tensor(part_m[:, m % 2, :], gate_m[:, m % 2, :], bank[b + 3][:, 0:T], ALU.mult))
                link(dve.tensor_tensor(part_s[:, m % 2, :], part_s[:, m % 2, :], rstd_row, ALU.mult))
                dve.tensor_tensor(mergedT[:, m, :], part_s[:, m % 2, :], part_m[:, m % 2, :], ALU.add
                                  ).then_inc(S["merged"], 1)
            dve.wait_ge(chunk_used, USED_MIXER)
            for c in range(3):
                for half in range(2):
                    i = dve.tensor_tensor(hid[0:rows(c), c, hb(c, half)], hid[0:rows(c), c, hb(c, half)],
                                          bank[2 * c + half][0:rows(c), :], ALU.add)
                i.then_inc(S["h_ready"], 1)
            for c in range(3):
                dve.wait_ge(S["h_ss"], c + 1)
                var(small[0:rows(c), 16 + c:17 + c], c, D).then_inc(S["h_var"], 1)
            dve.wait_ge(moe_in, 96)
            for c in range(3):
                dve.wait_ge(S["h_std"], c + 1)
                link(dve.reciprocal(small[0:rows(c), 12 + c:13 + c], small[0:rows(c), 20 + c:21 + c]))
                dve.scalar_tensor_tensor(hf[0:rows(c), c, :], hid[0:rows(c), c, :], small[0:rows(c), 12 + c:13 + c],
                                         nf_row[0:rows(c)], ALU.mult, ALU.mult).then_inc(S["hf_ready"], 1)
            link(dve.tensor_copy(bgu_parts[0:E, :], bgu[0:E, :]))
            link(dve.tensor_tensor(bgu_rest[0:E, :], bgu[0:E, :], bgu_parts[0:E, :], ALU.subtract))
            link(dve.tensor_copy(bgu_parts[E:2 * E, :], bgu_rest[0:E, :]))
            link(dve.tensor_copy(bgu[0:E, :], bgu_parts[E:2 * E, :]))
            link(dve.tensor_tensor(bgu_parts[2 * E:3 * E, :], bgu_rest[0:E, :], bgu[0:E, :], ALU.subtract))
            BIG = 3.0e38
            dve.wait_ge(S["lg_psum"], 1)
            link(dve.memset(logits[:, :, E:E + 4], BIG))
            for c in range(3):
                r = rows(c)
                link(dve.tensor_tensor(logits[0:r, c, 0:E], bank[0][0:r, c * H:c * H + E], br_row[0:r], ALU.add))
                link(dve.max(best[0:r, c, :], logits[0:r, c, 0:E]))
                link(dve.tensor_scalar(small[0:r, 24 + c:25 + c], best[0:r, c, 0:1], -1.0, None, ALU.mult))
                link(dve.memset(best[0:r, c, 4:8], BIG))
                dve.sem_inc(S["lg_ready"], 1)
                link(dve.match_replace(swept[0:r, c, :], best[0:r, c, :], logits[0:r, c, :], -BIG))
                link(dve.tensor_tensor(chosen[0:r, c, :], swept[0:r, c, 0:E], logits[0:r, c, 0:E], ALU.not_equal))
                dve.wait_ge(S["ge_ready"], c + 1)
                link(dve.scalar_tensor_tensor(gates[0:r, c, :], expd[0:r, c, :], 1.0, chosen[0:r, c, :],
                                              ALU.mult, ALU.mult))
                link(dve.reduce_sum(small[0:r, 50 + c:51 + c], gates[0:r, c, :], AX.X))
                link(dve.reciprocal(small[0:r, 54 + c:55 + c], small[0:r, 50 + c:51 + c]))
                dve.tensor_scalar(gates[0:r, c, :], gates[0:r, c, :], small[0:r, 54 + c:55 + c], None, ALU.mult
                                  ).then_inc(S["route_ready"], 1)
            dve.wait_ge(S["rank_psum"], 1)
            for c in range(3):
                r = rows(c)
                link(dve.scalar_tensor_tensor(slot_no[0:r, c, :], bank[1][0:r, c * H:c * H + E], 1.0,
                                              chosen[0:r, c, :], ALU.add, ALU.mult))
                link(dve.tensor_scalar(slot_no[0:r, c, :], slot_no[0:r, c, :], -1.0, None, ALU.add))
            dve.sem_inc(S["slot_ready"], 1)

            def select(n, e, first):
                if not isinstance(n, int) or n:
                    dve.wait_ge(S["xe_psum"], n)
                for c in range(3):
                    r = rows(c)
                    i = dve.tensor_scalar(take[0:r, c, :], slots[0:r, bass.ds(first, P)],
                                          slot_no[0:r, c, bass.ds(e, 1)], None, ALU.is_equal)
                i.then_inc(S["sel_ready"], 1)

            def weigh(n, e, first):
                if not isinstance(n, int) or n:
                    dve.wait_ge(S["gu_psum"], n * 4)
                    dve.wait_ge(S["gv_psum"], n)
                dve.tensor_scalar(pick_bias[:, :], row_expert[:, :], slots[0:96, bass.ds(e, 1)], None,
                                  ALU.is_equal).then_inc(S["bias_ready"], 1)
                for c in range(3):
                    r = rows(c)
                    i = dve.tensor_scalar(give[0:r, c, :], slots[0:r, bass.ds(first, P)],
                                          slot_no[0:r, c, bass.ds(e, 1)], gates[0:r, c, bass.ds(e, 1)],
                                          ALU.is_equal, ALU.mult)
                i.then_inc(S["give_ready"], 1)

            def swiglu(n):
                for q in range(4):
                    v = bank[q][:, :].rearrange("p (f two) -> p f two", two=2)
                    dve.wait_ge(S["gu_psum"], n * 4 + (q + 1))
                    dve.tensor_scalar(glu[:, q, :], v[:, :, 0], LIMIT, None, ALU.min).then_inc(S["glu_ready"], 1)
                    dve.tensor_scalar(lin[:, q, :], v[:, :, 1], -LIMIT, LIMIT, ALU.max, ALU.min
                                      ).then_inc(S["lin_ready"], 1)
                for q in range(4):
                    dve.wait_ge(S["lin_ready"], n * 4 + 4)
                    dve.scalar_tensor_tensor(lin[:, q, :], lin[:, q, :], 1.0, glu[:, q, :], ALU.add, ALU.mult
                                             ).then_inc(S["prod_ready"], 1)
                for q in range(4):
                    dve.wait_ge(S["prod_ready"], n * 4 + 4)
                    dve.wait_ge(S["sig_ready"], n * 4 + (q + 1))
                    dve.tensor_tensor(lin[:, q, :], lin[:, q, :], sig[:, q, :], ALU.mult
                                      ).then_inc(S["act_ready"], 1)

            def add_up(n):
                for i in range(6):
                    c, half = i // 2, i % 2
                    dve.wait_ge(S["cm_psum"], n * 6 + (i + 1))
                    dve.tensor_tensor(hid[0:rows(c), c, hb(c, half)], hid[0:rows(c), c, hb(c, half)],
                                      bank[4 + i % 2][0:rows(c), :], ALU.add).then_inc(S["cm_done"], 1)

            select(0, 0, 0)
            wlink = chain(dve, work_chain)
            dve.wait_ge(S["cnt_psum"], 1)
            for i in range(2):
                wlink(dve.tensor_scalar(flags[0:1, i, :], bank[2][0:1, 0:E], float(P * (i + 1)), None, ALU.is_gt))
            f = flags[0:1].rearrange("p a b -> p (a b)")
            wlink(dve.tensor_tensor_scan(ranks[0:1], ones[0:1, 0:2 * E], f, 0.0, ALU.mult, ALU.add))
            wlink(dve.tensor_tensor(match[0:1], ranks[0:1].unsqueeze(1).to_broadcast([1, MAX_EXTRA, 2 * E]),
                                    slots[0:1, 1:1 + MAX_EXTRA].unsqueeze(2).to_broadcast([1, MAX_EXTRA, 2 * E]),
                                    ALU.is_equal))
            wlink(dve.tensor_tensor(match[0:1], match[0:1], f.unsqueeze(1).to_broadcast([1, MAX_EXTRA, 2 * E]),
                                    ALU.mult))
            wlink(dve.tensor_tensor(match[0:1], match[0:1],
                                    slots[0:1, 0:2 * E].unsqueeze(1).to_broadcast([1, MAX_EXTRA, 2 * E]), ALU.mult))
            wlink(dve.reduce_sum(codes[0:1, 0:MAX_EXTRA], match[0:1], AX.X))
            wlink(dve.tensor_copy(work[0:1, 48:48 + MAX_EXTRA], codes[0:1, 0:MAX_EXTRA]))
            wlink(dve.tensor_copy(work[0:1, 32:33], ranks[0:1, 2 * E - 1:2 * E]))
            wlink(dve.tensor_scalar(work[0:1, 0:MAX_EXTRA], work[0:1, 48:48 + MAX_EXTRA], E - 1, None,
                                    ALU.bitwise_and))
            wlink(dve.tensor_scalar(work[0:1, 16:16 + MAX_EXTRA], work[0:1, 48:48 + MAX_EXTRA], 5, 7,
                                    ALU.logical_shift_right, ALU.logical_shift_left))
            dve.sem_inc(S["work_ready"], 1)
            for n in range(6):
                c, half = n // 2, n % 2
                dve.wait_ge(S["bd_psum"], n + 1)
                dve.tensor_tensor(hid[0:rows(c), c, hb(c, half)], hid[0:rows(c), c, hb(c, half)],
                                  bank[4 + n % 2][0:rows(c), :], ALU.add).then_inc(S["bd_done"], 1)

            def block_of(n, first=False, last=False):
                weigh(n, n, 0)
                if not last:
                    select(n + 1, n + 1, 0)
                swiglu(n)
                if not first:
                    add_up(n - 1)

            block_of(0, first=True)
            with dve.Fori(1, E - 1) as n:
                block_of(n)
            block_of(E - 1, last=True)
            add_up(E - 1)
            dve.wait_ge(S["cm_done"], 6 * E)
            more = dve.value_load(work[0:1, 32:33], min_val=0, max_val=MAX_EXTRA)
            with dve.If(more > 0):
                with dve.Fori(0, more) as i:
                    n = i + E
                    e = dve.value_load(work[0:1, bass.ds(i, 1)], min_val=0, max_val=E - 1)
                    b = dve.value_load(work[0:1, bass.ds(i + 16, 1)], min_val=0, max_val=P)
                    select(n, e, b + P)
                    weigh(n, e, b + P)
                    swiglu(n)
                    add_up(n)
                    dve.wait_ge(S["cm_done"], n * 6 + 6)
            dve.sem_inc(S["all_added"], 1)
            for c in range(3):
                dve.wait_ge(S["y_ss"], c + 1)
                var(small[0:rows(c), 28 + c:29 + c], c, D).then_inc(S["y_var"], 1)
            for c in range(3):
                dve.wait_ge(S["y_std"], c + 1)
                link(dve.reciprocal(small[0:rows(c), 12 + c:13 + c], small[0:rows(c), 32 + c:33 + c]))
                dve.scalar_tensor_tensor(hid[0:rows(c), c, :], hid[0:rows(c), c, :], small[0:rows(c), 12 + c:13 + c],
                                         nl_row[0:rows(c)], ALU.mult, ALU.mult).then_inc(S["y_out"], 1)


_INS = ["x_prompt", "x_sample", "state_conv", "state_ssm", "norm_mix", "w_in", "conv_w", "conv_b", "dt_bias",
        "a_log", "d_skip", "gnorm_w", "v_norm_w", "v_norm_b", "w_spatial", "b_spatial", "w_branch_ssd",
        "w_branch_mlp", "w_out", "norm_ffn", "w_router", "b_router", "w_gu", "b_gu", "w_down", "b_down",
        "norm_final"]
_OUTS = [(1, SEQ, D), (DB, DS, D), (1, 1, KEEP, CONV), (1, 1, H, HP, N), (1, DB, KEEP, CONV),
         (1, DB, H, HP, N), (1, DB, DS, D)]


def kernel(**inputs):
    import numpy as np
    import concourse.bacc as bacc
    from concourse.bass_utils import run_bass_kernel_spmd

    nc = bacc.Bacc("TRN2", target_bir_lowering=False, num_devices=1)
    arrays, args = {}, []
    for name in _INS:
        a = np.ascontiguousarray(inputs[name])
        arrays[f"in_{name}"] = a
        args.append(nc.dram_tensor(f"in_{name}", a.shape, mybir.dt.from_np(a.dtype), kind="ExternalInput").ap())
    for i, shape in enumerate(_OUTS):
        args.append(nc.dram_tensor(f"out_{i}", shape, F32, kind="ExternalOutput").ap())
    build(nc, *args)
    r = run_bass_kernel_spmd(nc, [arrays], core_ids=[0])
    return tuple(r.results[0][f"out_{i}"] for i in range(len(_OUTS)))
```

```python
from contextlib import ExitStack

import concourse.bass as bass
from concourse import mybir

ALU = mybir.AluOpType
ACT = mybir.ActivationFunctionType
F32 = mybir.dt.float32
I32 = mybir.dt.int32
BF16 = mybir.dt.bfloat16
F32R = mybir.dt.float32r
AX = mybir.AxisListType

P = 128
D = 1024
KD = D // P
SEQ, DB, DS = 256, 8, 8
NS = DB * DS
T = SEQ + NS
TILES = [(0, P), (P, P), (SEQ, NS)]
DI = 2 * D
H, HP, G, N = 32, 64, 4, 128
PAIRS = DI // P
CONV = DI + 2 * G * N
CT = CONV // P
TAPS = 4
CG = 6
KEEP = TAPS - 1
STATE_ROWS = KEEP * (1 + DB)
SPAN = KEEP + SEQ
STEP = KEEP + DS
GH = 8
E, TOPK, FF = 32, 4, 1024
LIMIT, ALPHA = 7.0, 1.702
EPS = 1e-5
Z0, X0, DT0 = 0, DI, DI + CONV
U0 = DT0 + H
V0 = U0 + D
GS0 = V0 + D
GM0 = GS0 + D
RING = 6
SLOT = 2048
SPLITS = 4
LEAD = SPLITS - 1
ON_POOL = (2, 5, 8)
EXPERT_CHUNKS = 12
MAX_EXTRA = T * TOPK // P


def mixer_chunks():
    out = [("v", m) for m in range(4)] + [("u", m) for m in range(4)] + [("dt", 0)]
    for g in range(G):
        out += [("x", 2 * g), ("x", 2 * g + 1), ("bc", g), ("z", 2 * g), ("z", 2 * g + 1)]
    for m in range(4):
        out += [("gs", m), ("bs", 2 * m), ("bs", 2 * m + 1), ("gm", m), ("bm", m)]
    return out + [("out", m) for m in range(4)]


CHUNKS = mixer_chunks()
AT = {c: n for n, c in enumerate(CHUNKS)}
N_MIXER = len(CHUNKS)
N_PROJ = AT[("gs", 0)]
USED_MIXER = N_MIXER - N_PROJ


def tiles_through(n):
    return sum(1 if c[0] == "dt" else 2 for c in CHUNKS[:n + 1])


def slot_of(j):
    return (N_MIXER + j) % RING


def slot_uses(slot, before):
    return sum(1 for n in range(before) if n % RING == slot)


def build(nc, x_prompt, x_sample, state_conv, state_ssm, norm_mix, w_in, conv_w, conv_b, dt_bias, a_log,
          d_skip, gnorm_w, v_norm_w, v_norm_b, w_spatial, b_spatial, w_branch_ssd, w_branch_mlp, w_out,
          norm_ffn, w_router, b_router, w_gu, b_gu, w_down, b_down, norm_final,
          y_prompt, y_sample, conv_prompt_new, ssm_prompt_new, conv_sample_new, ssm_sample_new, v_sample_new):
    ctx = ExitStack()
    with ctx:
        def sb(name, shape, dt=F32):
            return ctx.enter_context(nc.sbuf_tensor(name, shape, dt))

        def sem(name):
            return ctx.enter_context(nc.semaphore(name))

        with nc.sbuf_tensor("ring", [P, RING, SLOT], F32) as ring:
            pass
        ring_r = sb("ring_r", [P, RING, SLOT], F32R)
        hid = sb("hid", [P, 3, D])
        ident = sb("ident", [P, P])
        ones = sb("ones", [P, P])
        before = sb("before", [P, P])
        causal = sb("causal", [P, T])
        samebatch = sb("samebatch", [P, DB])
        ident_bf = sb("ident_bf", [P, P], BF16)
        repeat = sb("repeat", [DS, NS])
        running = sb("running", [H, T])
        slots_i = sb("slots_i", [P, 3 * P], I32)
        slots = sb("slots", [P, 3 * P])
        small = sb("small", [P, 64])
        bgu_parts = sb("bgu_parts", [96, 2 * FF], BF16)
        pick_bias = sb("pick_bias", [96, P], BF16)
        row_expert = sb("row_expert", [96, P])
        work = sb("work", [1, 64], I32)
        arena_size = 34576
        tail = arena_size - 2424
        with nc.sbuf_tensor("arena", [P, arena_size], F32) as arena:
            pass
        top = [0]

        def rounded(at, n):
            with ExitStack() as over:
                if at:
                    over.enter_context(nc.sbuf_tensor(f"below_{at}_{n}", [P, at], F32))
                return over.enter_context(nc.sbuf_tensor(f"rounded_{at}_{n}", [P, n], F32R))

        def place(at, *shape, parts=False):
            n = 1
            for s in shape:
                n *= s
            top[0] = at + n
            assert top[0] <= arena_size, (at, shape)
            v = rounded(at, n)[:, 0:n] if parts else arena[:, at:at + n]
            if len(shape) == 2:
                v = v.rearrange("p (a b) -> p a b", a=shape[0])
            if len(shape) == 3:
                v = v.rearrange("p (a b c) -> p a b c", a=shape[0], b=shape[1])
            return v

        def after(*shape):
            return place(top[0], *shape)

        def after_r(*shape):
            return place(top[0], *shape, parts=True)

        hnT = place(0, KD, T)
        mlpT = after(KD, T)
        base = top[0]
        hn = place(base, 3, D)
        vtok = after(3, D)
        csin = after(CONV)
        vT = after(2, T)
        vw_row = after(D)
        vb_row = after(D)
        nm_row = after(D)
        ws_in = after(GH, P)
        wsT = after(GH, P)
        wsS = after(GH, NS)
        bs_row = after(GH, P)
        junk = after(D)
        yT = place(base, PAIRS, T)
        csout = after(CONV)
        raw = after(2, SPAN + DB * STEP)
        acc = after(2, T)
        pack = after(CG, STATE_ROWS)
        xsT = [after(4, T) for _ in range(2)]
        bcT = [after(2, T) for _ in range(2)]
        cbm = after(T)
        btok = after(3, P)
        b_hi = after_r(N)
        b_lo = after_r(N)[0:NS]
        bmask_hi = after_r(DB, N)
        bmask_lo = after_r(DB, N)[0:NS]
        xs = after_r(2, P)
        vec_start = top[0]
        s_in = [after(DB, N) for _ in range(2)]
        s_T = [after(DB, P) for _ in range(2)]
        s_new = after(DB, N)
        s_fin = after(2, N)
        s_0T = after(2, P)
        xdt = after(2, 3 * P)
        xw = after(2, 3 * P)
        xf = after(2, P)
        seg = after(2, T)
        dec = after(2, T)
        esb = after(2, T - P)
        off = after(T - P)
        ysum = after(T)
        ssd_top = top[0]
        dtmp = place(vec_start + 4 * DB * N, 8, T)
        prefix = place(tail, CT, KEEP * DB)
        acumT = after(T)
        eacT = after(T)
        convv = after(CT * (TAPS + 1))
        gn_col = after(PAIRS)
        ds_col = after(PAIRS)
        tm = after(4, 3 * H)
        head_parts = after_r(2, T)[0:2 * H]
        pick_head = after_r(H)[0:2 * H]
        assert ssd_top <= tail, ssd_top
        mergedT = place(base + PAIRS * T, KD, T)
        gate_s = after(2, T)
        gate_m = after(2, T)
        part_s = after(2, T)
        part_m = after(2, T)
        rstd_row = after(T)
        branch_top = top[0]
        hn_lo = place(0, KD, T, parts=True)
        mlp_lo = after_r(KD, T)
        y_lo = place(base, PAIRS, T, parts=True)
        top[0] = branch_top
        hn_hi = after_r(KD, T)
        mlp_hi = after_r(KD, T)
        wb_hi = after_r(2, SLOT)
        y_hi = after_r(PAIRS, T)
        sqacc = place(tail - T, T)
        sq = place(tail - 2 * T, T)
        assert ssd_top <= tail - 2 * T, ssd_top
        hfb = sb("hfb", [P, 3, 3, D], BF16)
        nl_row = sb("nl_row", [P, D])
        routing = sb("routing", [P, 2400])
        cursor = [0]

        def part(*shape):
            n = 1
            for d in shape:
                n *= d
            v = routing[:, cursor[0]:cursor[0] + n]
            cursor[0] += n
            assert cursor[0] <= 2400
            return v.rearrange("p (a b) -> p a b", a=shape[0]) if len(shape) == 2 else v

        wr = part(KD, E)
        br_row = part(E)
        logits = part(3, E + 4)
        swept = part(3, E + 4)
        expd = part(3, E)
        best = part(3, 8)
        chosen = part(3, E)
        gates = part(3, E)
        gates_rest = part(3, E)
        slot_no = part(3, E)
        gate_of = part(4)
        gatesT = part(T)
        flags = part(2, E)
        ranks = part(2 * E)
        match = routing[:, 1600:1600 + MAX_EXTRA * 2 * E].rearrange("p (a b) -> p a b", a=MAX_EXTRA)
        codes = routing[:, 2300:2316]
        assert cursor[0] <= 1600
        gates3 = sb("gates3", [P, 3, E, 3], BF16)
        take = sb("take", [P, 3, P], BF16)
        kept = sb("kept", [P, 3, P], BF16)
        takeT = sb("takeT", [P, 3 * P], F32R)
        xe_hi = sb("xe_hi", [P, KD, P], F32R)
        xe_lo = sb("xe_lo", [P, KD, P], F32R)
        swi = sb("swi", [P, 3, 4, FF // 4])
        glu, lin, sig = swi[:, 0], swi[:, 1], swi[:, 2]
        act_hi = sb("act_hi", [P, KD, P], F32R)
        act_lo = sb("act_lo", [P, KD, P], F32R)
        ye_hi = sb("ye_hi", [P, D], F32R)
        ye_lo = sb("ye_lo", [P, D], F32R)
        junk2 = swi[:, 0:1].rearrange("p a b c -> p (a b c)")
        bd = swi[:, 1:2].rearrange("p a b c -> p (a b c)")
        router_memory = ExitStack()
        early = router_memory.enter_context(nc.sbuf_tensor("early", [P, 3 * D + 3 * D + KD * T + D + 2 * FF], F32))
        hf = early[:, 0:3 * D].rearrange("p (c d) -> p c d", c=3)
        hf_rest = early[:, 3 * D:6 * D].rearrange("p (c d) -> p c d", c=3)
        hfT = early[:, 6 * D:6 * D + KD * T].rearrange("p (k t) -> p k t", k=KD)
        nf_row = early[:, 6 * D + KD * T:7 * D + KD * T]
        bgu = early[:, 7 * D + KD * T:9 * D + KD * T]
        bgu_rest = early[:, 6 * D:6 * D + 2 * FF]
        router_memory.close()
        w_hi = sb("w_hi", [P, SPLITS, SLOT], F32R)
        w_lo = sb("w_lo", [P, SPLITS, SLOT], F32R)

        bank = [ctx.enter_context(nc.psum_tensor(f"bank{i}", [P, 512], F32)) for i in range(8)]

        slot_full = [sem(f"slot_full{i}") for i in range(RING)]
        chunk_used = sem("chunk_used")
        x_in = sem("x_in")
        rows_in = sem("rows_in")
        vecs_in = sem("vecs_in")
        csin_in = sem("csin_in")
        ws_in_s = sem("ws_in_s")
        heads_in = sem("heads_in")
        moe_in = sem("moe_in")
        bd_in = sem("bd_in")
        consts = sem("consts")
        pool_chain = sem("pool_chain")
        act_chain = sem("act_chain")
        dve_chain = sem("dve_chain")
        stored = sem("stored")

        block = ctx.enter_context(nc.Block())
        names = ("x_ss", "x_var", "x_std", "hn_ready", "hnT_psum", "hnT_ready", "vec_psum", "vec_ready",
                 "pre_psum", "pre_ready", "proj_ready", "proj_read", "vT_ready", "vt_psum", "vt_ready",
                 "ln_var", "ln_std", "v_ready", "ws_psum", "ws_ready", "mix_psum", "mix_read",
                 "dt_exp", "dt_abs", "dt_ln", "dt_u", "acum_ready", "dt_w", "tm_psum", "tm_ready",
                 "raw_ready", "pre_copied", "conv_done", "packed", "conv_act", "cs_psum", "cs_ready",
                 "cb_psum", "cb_ready", "bt_psum", "bt_ready", "bm_ready", "xt_psum", "xw_ready", "xs_hi", "xs_ready",
                 "head_psum", "seg_ready", "exp_ready", "decay_ready", "e_psum", "e_ready",
                 "sT_psum", "sT_ready", "s0_ready", "sf_psum", "sf_ready", "sn_psum", "sn_ready",
                 "off_psum", "off_read", "yd_psum", "y_ready", "sq_ready", "sq_psum", "rs_var", "rs_std",
                 "rs_ready", "gates_ready", "merged", "out_psum", "h_ready", "h_ss", "h_var", "h_std",
                 "hf_ready", "hfT_psum", "hfT_ready", "lg_psum", "lg_ready", "ge_ready", "route_ready",
                 "branch_hi", "branch_lo", "bgu_ready", "cnt_psum", "rank_psum", "slot_ready", "work_ready", "bd_psum", "bd_done", "gT_psum", "gT_ready",
                 "sel_ready", "xe_psum", "xe_ready", "gu_psum", "glu_ready", "sig_ready", "act_ready", "at_psum",
                 "at_ready", "ye_ready", "cm_psum", "cm_done",
                 "y_ss", "y_var", "y_std", "y_out",
                 "bias_ready", "hi_ready", "lo_dve", "lo_pool", "early_done", "parts_hi", "parts_rest", "kept_ready", "kept_used", "xe_lo_ready", "at_lo_ready",
                 "tk_psum", "tk_ready", "gate_ready", "ye_lo_ready", "lin_ready", "prod_ready", "all_added")
        S = {n: sem(n) for n in names}
        s_in_full = [sem("s_in_full0"), sem("s_in_full1")]
        s_fin_out = [sem("s_fin_out0"), sem("s_fin_out1")]
        s_new_out = sem("s_new_out")
        v_out = sem("v_out")
        cs_out = sem("cs_out")
        work_chain = sem("work_chain")

        def chain(eng, s):
            n = [0]

            def link(ins):
                n[0] += 1
                ins.then_inc(s, 1)
                eng.wait_ge(s, n[0])
            return link

        w_in_t = w_in[0].rearrange("(k p) n -> p k n", p=P)
        bs_t = w_branch_ssd[0].rearrange("(q k p) n -> q p k n", p=P, k=KD)
        bm_t = w_branch_mlp[0].rearrange("(k p) n -> p k n", p=P)
        out_t = w_out[0].rearrange("(m k p) n -> m p k n", p=P, k=2)
        gu_t = w_gu[0].rearrange("e (j p) n -> p e j n", p=P)
        down_t = w_down[0].rearrange("e (j k p) n -> j p e k n", p=P, k=2)

        def wide(n):
            return ring[:, n % RING, :].rearrange("p (k n) -> p k n", k=KD)

        def pair_rows(s):
            return ring[:, s, :].rearrange("p (k n) -> p k n", k=2)

        def parts_of(kind, m):
            n = AT[(kind, m)]
            if kind in ("u", "v", "x", "z", "gs", "gm"):
                c = {"u": U0, "v": V0, "x": X0, "z": Z0, "gs": GS0, "gm": GM0}[kind] + 256 * m
                return [(wide(n), w_in_t[:, :, c:c + 256])]
            if kind == "dt":
                return [(ring[:, n % RING, 0:KD * H].rearrange("p (k n) -> p k n", k=KD),
                         w_in_t[:, :, DT0:DT0 + H])]
            if kind == "bc":
                b = X0 + DI + m * N
                return [(wide(n)[:, :, 0:N], w_in_t[:, :, b:b + N]),
                        (wide(n)[:, :, N:2 * N], w_in_t[:, :, b + G * N:b + G * N + N])]
            if kind == "bs":
                return [(wide(n), bs_t[m % 2][:, :, 256 * (m // 2):256 * (m // 2) + 256])]
            if kind == "bm":
                return [(wide(n), bm_t[:, :, 256 * m:256 * m + 256])]
            return [(pair_rows(n % RING), out_t[m])]

        filled = [0] * RING
        full_at = []
        for c in CHUNKS:
            s = AT[c] % RING
            filled[s] += 16 * len(parts_of(*c))
            full_at.append(filled[s])

        def chunk_ready(pe, c):
            n = AT[c]
            pe.wait_ge(slot_full[n % RING], full_at[n])

        def expert_slot_ready(pe, n, j):
            s = slot_of(j)
            pe.wait_ge(slot_full[s], n * 32 + (filled[s] + 16 * (j // RING + 1)))

        def lo_made(eng, n, j):
            pool_j = sum(1 for i in ON_POOL if i <= j)
            if j in ON_POOL:
                eng.wait_ge(S["lo_pool"], n * len(ON_POOL) + pool_j)
            else:
                eng.wait_ge(S["lo_dve"], n * (EXPERT_CHUNKS - len(ON_POOL)) + (j + 1 - pool_j))

        def rows(c):
            return TILES[c][1]

        def tok(c):
            return slice(TILES[c][0], TILES[c][0] + TILES[c][1])

        def hb(c, half):
            return slice(half * 512, half * 512 + 512)

        Q_DT = 16
        xchan = lambda g, t: (4 * g + t) if t < 4 else (PAIRS + g if t == 4 else PAIRS + G + g)
        BRANCH = ([("hn", 0), ("w", 0)] + [("y", i) for i in range(4)] + [("w", 1), ("w", 2), ("mlp", 0)]
                  + [("w", i) for i in range(3, 20)])
        FIRST_BRANCH = AT[("gs", 0)]

        def branch_item(item):
            kind, i = item
            if kind == "w":
                slot = (FIRST_BRANCH + i) % RING
                return ring[:, slot, :], wb_hi[:, i % 2, :], ring_r[:, slot, :]
            if kind == "y":
                t = slice(4 * i, 4 * i + 4)
                return yT[:, t, :], y_hi[:, t, :], y_lo[:, t, :]
            return (hnT, hn_hi, hn_lo) if kind == "hn" else (mlpT, mlp_hi, mlp_lo)

        def branch_split(item):
            return BRANCH.index(item) + 1
        col_a, col_b = 0, 16

        @block.sync
        def _(sp):
            sp.dma_start(hid[:, 0:2, :], x_prompt[0].rearrange("(c p) d -> p c d", p=P)).then_inc(x_in, 16)
            sp.dma_start(hid[0:NS, 2, :], x_sample.rearrange("b l d -> (b l) d")).then_inc(x_in, 16)
            for n, c in enumerate(CHUNKS):
                if n >= RING:
                    if n - RING < N_PROJ:
                        sp.wait_ge(S["proj_ready"], tiles_through(n - RING))
                    else:
                        sp.wait_ge(chunk_used, n - RING - N_PROJ + 1)
                for dst, src in parts_of(*c):
                    sp.dma_start(dst, src).then_inc(slot_full[n % RING], 16)

            def load_expert(n, e):
                for j in range(EXPERT_CHUNKS):
                    s = slot_of(j)
                    if j >= RING:
                        lo_made(sp, n, j - RING)
                    elif isinstance(n, int) and n == 0:
                        sp.wait_ge(chunk_used, USED_MIXER + j - RING + 1)
                    else:
                        lo_made(sp, n + (-1), j - RING + EXPERT_CHUNKS)
                    if j < 8:
                        sp.dma_start(ring[:, s, :], gu_t[:, bass.ds(e, 1), j, :].rearrange("p e n -> p (e n)")
                                     ).then_inc(slot_full[s], 16)
                    else:
                        sp.dma_start(pair_rows(s), down_t[j - 8][:, bass.ds(e, 1), :, :].rearrange(
                            "p e k n -> p (e k) n")).then_inc(slot_full[s], 16)

            load_expert(0, 0)
            with sp.Fori(1, E) as e:
                load_expert(e, e)
            sp.wait_ge(S["work_ready"], 1)
            more = sp.value_load(work[0:1, 32:33], min_val=0, max_val=MAX_EXTRA)
            with sp.If(more > 0):
                with sp.Fori(0, more) as i:
                    e = sp.value_load(work[0:1, bass.ds(i, 1)], min_val=0, max_val=E - 1)
                    load_expert(i + E, e)

        @block.gpsimd
        def _(pool):
            link = chain(pool, pool_chain)
            pool.dma_start(nm_row, norm_mix[0].partition_broadcast(P)).then_inc(rows_in, 16)
            pool.dma_start(junk[0:96, 0:P], conv_w[0].rearrange("k (t p) -> (k t) p", p=P)).then_inc(vecs_in, 16)
            pool.dma_start(junk[96:120, 0:P], conv_b[0].rearrange("(t p) -> t p", p=P)).then_inc(vecs_in, 16)
            pool.dma_start(junk[0:PAIRS, P:2 * P], gnorm_w[0].rearrange("(t p) -> t p", p=P)).then_inc(vecs_in, 16)
            pool.dma_start(csin[0:KEEP * DB, :], state_conv[0].rearrange("b k c -> (b k) c")).then_inc(csin_in, 16)
            pool.dma_start(ws_in, w_spatial[0].rearrange("g t s -> t g s")).then_inc(ws_in_s, 16)
            pool.dma_start(bs_row[0:1], b_spatial[0:1]).then_inc(ws_in_s, 16)
            pool.dma_start(vw_row, v_norm_w[0].partition_broadcast(P)).then_inc(heads_in, 16)
            pool.dma_start(vb_row, v_norm_b[0].partition_broadcast(P)).then_inc(heads_in, 16)
            pool.dma_start(small[0:H, 0:1], dt_bias[0].unsqueeze(1)).then_inc(heads_in, 16)
            pool.dma_start(small[0:H, 1:2], a_log[0].unsqueeze(1)).then_inc(heads_in, 16)
            for half in range(2):
                pool.dma_start(ds_col[HP * half:HP * half + HP, :],
                               d_skip[0].rearrange("(j two) -> two j", two=2)[half].partition_broadcast(HP),
                               allow_slow_non_contiguous=True
                               ).then_inc(heads_in, 16)
            link(pool.memset(ident[:], 0.0))
            link(pool.affine_select(out=ident[:], in_=ident[:], compare_op=ALU.not_equal, fill=1.0, base=0,
                                    pattern=[[-1, P]], channel_multiplier=1))
            link(pool.tensor_copy(repeat[:].rearrange("p (b l) -> p b l", b=DB),
                                  ident[0:DS, 0:DS].unsqueeze(1).to_broadcast([DS, DB, DS])))
            link(pool.tensor_copy(ident_bf[:], ident[:]))
            for i in range(2):
                s = slice(i * H, i * H + H)
                link(pool.tensor_copy(pick_head[s, :], ident[s, s]))
            link(pool.memset(ones[:], 1.0))
            link(pool.affine_select(out=before[:], in_=ones[:], compare_op=ALU.is_ge, fill=0.0, base=-1,
                                    pattern=[[1, P]], channel_multiplier=-1))
            link(pool.memset(causal[:], 1.0))
            for c in range(2):
                link(pool.affine_select(out=causal[:, tok(c)], in_=causal[:, tok(c)], compare_op=ALU.is_ge,
                                        fill=0.0, base=0, pattern=[[1, P]], channel_multiplier=-1))
            link(pool.affine_select(out=causal[0:NS, SEQ:T], in_=causal[0:NS, SEQ:T], compare_op=ALU.is_ge,
                                    fill=0.0, base=0, pattern=[[1, NS]], channel_multiplier=-1))
            link(pool.affine_select(out=causal[0:NS, SEQ:T], in_=causal[0:NS, SEQ:T], compare_op=ALU.is_ge,
                                    fill=0.0, base=0, pattern=[[-DS, DB], [0, DS]], channel_multiplier=1))
            link(pool.memset(samebatch[:], 1.0))
            link(pool.affine_select(out=samebatch[0:NS], in_=samebatch[0:NS], compare_op=ALU.is_ge, fill=0.0,
                                    base=0, pattern=[[-DS, DB]], channel_multiplier=1))
            link(pool.affine_select(out=samebatch[0:NS], in_=samebatch[0:NS], compare_op=ALU.is_ge, fill=0.0,
                                    base=DS - 1, pattern=[[DS, DB]], channel_multiplier=-1))
            link(pool.tensor_copy(samebatch[NS:2 * NS], samebatch[0:NS]))
            link(pool.memset(running[:], 1.0))
            link(pool.memset(running[:, 0:SEQ:P], 0.0))
            link(pool.memset(running[:, SEQ:T:DS], 0.0))
            link(pool.iota(slots_i[:], pattern=[[1, 3 * P]], base=0, channel_multiplier=0))
            link(pool.tensor_copy(slots[:], slots_i[:]))
            for part in range(3):
                link(pool.iota(slots_i[32 * part:32 * part + 32, 0:P], pattern=[[0, P]], base=0,
                               channel_multiplier=1))
            pool.tensor_copy(row_expert[:], slots_i[0:96, 0:P]).then_inc(consts, 1)

            pool.wait_ge(S["mix_read"], GH)
            link(pool.memset(cbm, 0.0))
            for r in range(2):
                link(pool.memset(raw[:, r, 0:KEEP], 0.0))
            pool.wait_ge(S["pre_ready"], 2)

            def conv_group(g):
                for t in range(CG):
                    n = g * CG + t
                    r = raw[:, n % 2, SPAN:].rearrange("p (b k) -> p b k", k=STEP)
                    ch = xchan(g, t)
                    if n >= 2:
                        pool.wait_ge(S["conv_done"], n - 1)
                    pool.tensor_copy(r[:, :, 0:KEEP], prefix[:, ch, :].rearrange("p (b k) -> p b k", k=KEEP)
                                     ).then_inc(S["pre_copied"], 1)
                    if g >= 1 and t == 0:
                        pool.wait_ge(S["cs_psum"], g)
                    pool.wait_ge(S["raw_ready"], n + 1)
                    pool.tensor_copy(pack[:, t, 0:KEEP], raw[:, n % 2, SEQ:SEQ + KEEP])
                    pool.tensor_copy(pack[:, t, KEEP:].rearrange("p (b k) -> p b k", k=KEEP),
                                     r[:, :, DS:DS + KEEP]).then_inc(S["packed"], 1)

            def ssd_group(g):
                pool.wait_ge(S["bt_ready"], g + 1)
                if g:
                    pool.wait_ge(S["sn_psum"], 4 * g)
                pool.tensor_tensor(bmask_hi, b_hi.bitcast(F32).unsqueeze(1).to_broadcast([P, DB, N]),
                                   samebatch[:].unsqueeze(2).to_broadcast([P, DB, N]), ALU.mult)
                link(pool.tensor_tensor(b_lo, btok[0:NS, 2, :], b_hi[0:NS].bitcast(F32), ALU.subtract))
                pool.tensor_tensor(bmask_lo, b_lo.bitcast(F32).unsqueeze(1).to_broadcast([NS, DB, N]),
                                   samebatch[0:NS].unsqueeze(2).to_broadcast([NS, DB, N]), ALU.mult
                                   ).then_inc(S["bm_ready"], 1)
                def squares(j):
                    pool.wait_ge(S["y_ready"], j + 1)
                    if j == 0:
                        link(pool.tensor_tensor(sqacc, yT[:, j, :], yT[:, j, :], ALU.mult))
                    else:
                        link(pool.tensor_tensor(sq, yT[:, j, :], yT[:, j, :], ALU.mult))
                        link(pool.tensor_tensor(sqacc, sqacc, sq, ALU.add))
                    pool.tensor_scalar(yT[:, j, :], yT[:, j, :], gn_col[:, j:j + 1], None, ALU.mult
                                       ).then_inc(S["sq_ready"], 1)

                for j in range(4 * g, 4 * g + 4):
                    pool.wait_ge(S["exp_ready"], j + 1)
                    pool.wait_ge(S["cb_ready"], g + 1)
                    pool.tensor_tensor(dec, dec, cbm.unsqueeze(1).to_broadcast([P, 2, T]), ALU.mult
                                       ).then_inc(S["decay_ready"], 1)
                    if j > 4 * g:
                        squares(j - 1)
                squares(4 * g + 3)

            for step in range(G + 1):
                if step < G:
                    conv_group(step)
                else:
                    pool.wait_ge(S["cs_ready"], G)
                    pool.dma_start(conv_prompt_new[0, 0], csout[0:KEEP, :]).then_inc(cs_out, 16)
                    pool.dma_start(conv_sample_new[0].rearrange("b k c -> (b k) c"), csout[KEEP:STATE_ROWS, :]
                                   ).then_inc(cs_out, 16)
                if step:
                    ssd_group(step - 1)
            pool.wait_ge(S["merged"], 8)
            pool.wait_ge(s_new_out, 16 * PAIRS)
            pool.wait_ge(s_fin_out[0], 16 * PAIRS // 2)
            pool.wait_ge(s_fin_out[1], 16 * PAIRS // 2)
            pool.dma_start(nf_row, norm_ffn[0].partition_broadcast(P)).then_inc(moe_in, 16)
            pool.dma_start(wr, w_router[0].rearrange("(k p) e -> p k e", p=P)).then_inc(moe_in, 16)
            pool.dma_start(br_row, b_router[0].partition_broadcast(P)).then_inc(moe_in, 16)
            pool.dma_start(bgu[0:E, :], b_gu[0]).then_inc(moe_in, 16)
            pool.dma_start(nl_row[:], norm_final.partition_broadcast(P)).then_inc(moe_in, 16)
            pool.wait_ge(moe_in, 80)
            link(pool.tensor_copy(bgu_parts[0:E, :], bgu[0:E, :]))
            link(pool.tensor_tensor(bgu_rest[0:E, :], bgu[0:E, :], bgu_parts[0:E, :], ALU.subtract))
            link(pool.tensor_copy(bgu_parts[E:2 * E, :], bgu_rest[0:E, :]))
            link(pool.tensor_copy(bgu[0:E, :], bgu_parts[E:2 * E, :]))
            link(pool.tensor_tensor(bgu_parts[2 * E:3 * E, :], bgu_rest[0:E, :], bgu[0:E, :], ALU.subtract))
            pool.sem_inc(S["bgu_ready"], 1)
            pool.wait_ge(chunk_used, USED_MIXER)
            pool.dma_start(bd[0:E, :], b_down[0]).then_inc(bd_in, 16)
            link(pool.memset(takeT[:, T:].bitcast(F32), 0.0))
            pool.sem_inc(S["kept_used"], 1)

            def keep(n):
                pool.wait_ge(S["sel_ready"], n + 1)
                pool.wait_ge(S["kept_used"], n + 1)
                pool.tensor_tensor(kept[:, 0:2, :], take[:, 0:2, :], take[:, 0:2, :], ALU.mult)
                pool.tensor_tensor(kept[0:NS, 2, :], take[0:NS, 2, :], take[0:NS, 2, :], ALU.mult
                                   ).then_inc(S["kept_ready"], 1)

            def split_lo(n, j):
                pool.wait_ge(S["hi_ready"], n * EXPERT_CHUNKS + (j + 1))
                pool.tensor_tensor(w_lo[:, j % SPLITS, :], ring[:, slot_of(j), :],
                                   w_hi[:, j % SPLITS, :].bitcast(F32), ALU.subtract).then_inc(S["lo_pool"], 1)

            def block_of(n):
                keep(n)
                for j in ON_POOL:
                    split_lo(n, j)

            block_of(0)
            with pool.Fori(1, E) as n:
                block_of(n)
            pool.wait_ge(S["work_ready"], 1)
            more = pool.value_load(work[0:1, 32:33], min_val=0, max_val=MAX_EXTRA)
            with pool.If(more > 0):
                with pool.Fori(0, more) as i:
                    block_of(i + E)

        @block.tensor
        def _(pe):
            def turn(out, in_):
                return pe.transpose(out, in_, ident[0:in_.shape[0], 0:in_.shape[0]])

            def project(q, c, t, cols=P):
                if t == 0:
                    chunk_ready(pe, c)
                if q >= 2:
                    pe.wait_ge(S["proj_read"], q - 1)
                n = AT[c]
                for k in range(KD):
                    w = (ring[:, n % RING, k * H:k * H + H] if c[0] == "dt"
                         else wide(n)[:, k, t * P:t * P + P])
                    mm = pe.matmul(bank[q % 2][0:cols, 0:T], w, hnT[:, k, :], start=(k == 0), stop=(k == KD - 1))
                mm.then_inc(S["proj_ready"], 1)

            pe.wait_ge(consts, 1)
            pe.wait_ge(S["hn_ready"], 3)
            for k in range(KD):
                if k >= 2:
                    pe.wait_ge(S["hnT_ready"], k - 1)
                for c in range(3):
                    mm = turn(bank[k % 2][:, tok(c)], hn[0:rows(c), c, k * P:k * P + P])
                mm.then_inc(S["hnT_psum"], 1)
            pe.wait_ge(vecs_in, 48)
            turn(bank[2][:, 0:120], junk[0:120, 0:P])
            turn(bank[2][:, 120:120 + PAIRS], junk[0:PAIRS, P:2 * P]).then_inc(S["vec_psum"], 1)
            pe.wait_ge(csin_in, 16)
            for half in range(2):
                for i in range(CT // 2):
                    ch = half * CT // 2 + i
                    mm = turn(bank[3 + half][:, i * 24:i * 24 + 24], csin[0:KEEP * DB, ch * P:ch * P + P])
                mm.then_inc(S["pre_psum"], 1)
            pe.wait_ge(ws_in_s, 32)
            for g in range(GH):
                mm = turn(bank[5 + g // 4][:, (g % 4) * P:(g % 4) * P + P], ws_in[:, g, :])
            mm.then_inc(S["ws_psum"], 1)
            pe.wait_ge(S["ws_ready"], 1)
            pe.matmul(bank[7][0:NS, 0:GH * DS], repeat[:, :],
                      wsT[0:DS, :, 0:DS], start=True, stop=True).then_inc(S["ws_psum"], 1)

            def turn_v(m):
                pe.wait_ge(S["vT_ready"], m + 1)
                if m >= 2:
                    pe.wait_ge(S["vt_ready"], m - 1)
                if m == 0:
                    pe.wait_ge(S["vec_ready"], 1)
                if m == 1:
                    pe.wait_ge(S["pre_ready"], 2)
                for c in range(3):
                    mm = turn(bank[2 + m % 2][0:rows(c), c * P:c * P + P], vT[:, m % 2, tok(c)])
                mm.then_inc(S["vt_psum"], 1)

            pe.wait_ge(S["hnT_ready"], KD)
            for m in range(8):
                project(m, ("v", m // 2), m % 2)
                if m:
                    turn_v(m - 1)
            turn_v(7)
            for m in range(8):
                project(8 + m, ("u", m // 2), m % 2)
            project(Q_DT, ("dt", 0), 0, H)

            pe.wait_ge(S["v_ready"], 3)
            pe.wait_ge(S["ws_ready"], 2)
            for g in range(GH):
                b = bank[4 + g % 2]
                if g >= 2:
                    pe.wait_ge(S["mix_read"], g - 1)
                if g == 0:
                    pe.wait_ge(S["pre_ready"], 2)
                for c in range(3):
                    w = wsT[:, g, :] if c < 2 else wsS[0:NS, g, :]
                    pe.matmul(b[:, tok(c)], vtok[0:rows(c), c, g * P:g * P + P], w, start=True, stop=False)
                    bias = (bs_row[0:1, g, :] if c < 2
                            else bs_row[0:1, g, 0:DS].unsqueeze(1).to_broadcast([1, DB, DS]))
                    mm = pe.matmul(b[:, tok(c)], ones[0:1, :], bias, start=False, stop=True)
                mm.then_inc(S["mix_psum"], 1)

            pe.wait_ge(S["dt_w"], 1)
            for kind, src in enumerate((0, None, 3, 4)):
                for c in range(3 if kind < 3 else 1):
                    v = acumT[0:H, tok(c)] if src is None else dtmp[0:H, src, tok(c)]
                    mm = turn(bank[2][0:rows(c), kind * 96 + c * H:kind * 96 + c * H + H], v)
            mm.then_inc(S["tm_psum"], 1)

            def conv_group(g):
                q = Q_DT + 1 + 10 * g
                if g:
                    pe.wait_ge(S["sn_ready"], 4 * g - 4)
                for t in range(CG):
                    project(q + t, ("x", 2 * g + t // 2) if t < 4 else ("bc", g), t % 2)
                for t in range(4):
                    project(q + CG + t, ("z", 2 * g + t // 2), t % 2)
                pe.wait_ge(S["packed"], CG * (g + 1))
                if g >= 2:
                    pe.wait_ge(S["xw_ready"], 4 * g - 4)
                    pe.wait_ge(S["seg_ready"], 4 * g - 4)
                else:
                    pe.wait_ge(S["tm_ready"], 1)
                    pe.wait_ge(S["mix_read"], GH)
                    if g == 1:
                        pe.wait_ge(S["cs_ready"], 1)
                for t in range(CG):
                    o = bank[2][0:STATE_ROWS, t * P:t * P + P] if t < 4 else \
                        bank[4][0:STATE_ROWS, (t - 4) * P:(t - 4) * P + P]
                    mm = turn(o, pack[:, t, :])
                mm.then_inc(S["cs_psum"], 1)

            def ssd_group(g):
                x, bc = xsT[g % 2], bcT[g % 2]
                pe.wait_ge(S["conv_act"], CG * (g + 1))
                if g:
                    pe.wait_ge(S["y_ready"], 4 * g)
                    pe.wait_ge(S["s0_ready"], 4 * g)
                    pe.wait_ge(S["sf_ready"], 4 * g)
                else:
                    pe.wait_ge(S["ws_ready"], 2)
                for c in range(3):
                    mm = pe.matmul(bank[7][0:rows(c), tok(c)], bc[:, 0, tok(c)], bc[:, 1, tok(c)],
                                   start=True, stop=True)
                mm.then_inc(S["cb_psum"], 1)
                for c in range(3):
                    mm = turn(bank[6][0:rows(c), c * P:c * P + P], bc[:, 0, tok(c)])
                mm.then_inc(S["bt_psum"], 1)
                pe.wait_ge(S["cs_ready"], min(g + 2, G))

                def turn_x(jj):
                    if 4 * g + jj:
                        pe.wait_ge(S["xw_ready"], 4 * g + jj)
                    for c in range(3):
                        mm = turn(bank[2][0:rows(c), c * P:c * P + P], x[:, jj, tok(c)])
                    mm.then_inc(S["xt_psum"], 1)

                turn_x(0)
                for jj in range(4):
                    j = 4 * g + jj
                    p = j % 2
                    if j:
                        pe.wait_ge(S["seg_ready"], j)
                    for hh in range(2):
                        h = 2 * j + hh
                        mm = pe.matmul(bank[3 + hh][:, 0:T], pick_head[:, h:h + 1].to_broadcast([2 * H, P]),
                                       head_parts[:, 0, :], start=True, stop=True)
                    mm.then_inc(S["head_psum"], 1)
                    if j:
                        pe.wait_ge(S["e_ready"], j)
                        pe.wait_ge(S["off_read"], j)
                    for hh in range(2):
                        h = 2 * j + hh
                        mm = pe.matmul(bank[5][:, (T - P) * hh:(T - P) * hh + T - P],
                                       pick_head[:, h:h + 1].to_broadcast([2 * H, P]), head_parts[:, 1, P:T],
                                       start=True, stop=True)
                    mm.then_inc(S["e_psum"], 1)
                    pe.wait_ge(s_in_full[p], 16 * (j // 2 + 1))
                    if j:
                        pe.wait_ge(S["sn_ready"], j)
                    pe.wait_ge(S["proj_read"], Q_DT + 1 + 10 * min(g + 2, G))
                    for b in range(DB):
                        mm = turn(bank[b // 4][:, (b % 4) * P:(b % 4) * P + P], s_in[p][:, b, :])
                    mm.then_inc(S["sT_psum"], 1)
                    pe.wait_ge(S["bt_ready"], g + 1)
                    pe.wait_ge(S["xw_ready"], j + 1)
                    if j:
                        pe.wait_ge(S["s0_ready"], j)
                        pe.wait_ge(S["sf_ready"], j)
                    pe.matmul(bank[6][:, 0:P], btok[:, 0, :], xw[:, p, 0:P], start=True, stop=True)
                    pe.matmul(bank[6][:, P:2 * P], xf[:, p, :], btok[:, 0, :], start=True, stop=False)
                    pe.matmul(bank[6][:, P:2 * P], xw[:, p, P:2 * P], btok[:, 1, :], start=False, stop=True
                              ).then_inc(S["sf_psum"], 1)
                    pe.wait_ge(S["bm_ready"], g + 1)
                    pe.wait_ge(S["xs_ready"], j + 1)
                    for half in range(2):
                        pe.wait_ge(S["sT_ready"], 2 * j + (half + 1))
                        s4 = slice(4 * half, 4 * half + 4)
                        pe.matmul(bank[half][:, :], xs[:, p, :], bmask_hi[:, s4, :], start=True, stop=False)
                        mm = pe.matmul(bank[half][:, :], xs[0:NS, p, :], bmask_lo[:, s4, :], start=False, stop=True)
                    mm.then_inc(S["sn_psum"], 1)
                    if jj < 3:
                        turn_x(jj + 1)
                    pe.wait_ge(S["s0_ready"], j + 1)
                    pe.wait_ge(S["e_ready"], j + 1)
                    pe.matmul(bank[5][:, T - P:T], s_0T[:, p, :], bc[:, 1, P:2 * P], start=True, stop=True)
                    for b in range(DB):
                        mm = pe.matmul(bank[5][:, T + DS * b:T + DS * b + DS], s_T[p][:, b, :],
                                       bc[:, 1, SEQ + DS * b:SEQ + DS * b + DS], start=True, stop=True)
                    mm.then_inc(S["off_psum"], 1)
                    pe.wait_ge(S["decay_ready"], j + 1)
                    pe.wait_ge(S["cb_ready"], g + 1)
                    if j:
                        pe.wait_ge(S["y_ready"], j)
                    for hh in range(2):
                        for c in range(3):
                            mm = pe.matmul(bank[7][HP * hh:HP * hh + HP, tok(c)],
                                           xdt[0:rows(c), p, c * P + HP * hh:c * P + HP * hh + HP],
                                           dec[0:rows(c), hh, tok(c)], start=True, stop=True)
                    mm.then_inc(S["yd_psum"], 1)

            for step in range(G + 1):
                if step < G:
                    conv_group(step)
                if step:
                    ssd_group(step - 1)

            pe.wait_ge(S["sn_ready"], PAIRS)
            pe.wait_ge(S["seg_ready"], PAIRS)
            for mm2 in range(4):
                if mm2:
                    pe.wait_ge(S["gates_ready"], 2 * mm2)
                for which, c in enumerate((("gs", mm2), ("bs", 2 * mm2), ("bs", 2 * mm2 + 1), ("gm", mm2),
                                           ("bm", mm2))):
                    n = AT[c]
                    chunk_ready(pe, c)
                    if which == 1 and mm2:
                        pe.wait_ge(S["merged"], 2 * mm2)
                    elif which == 1:
                        pe.wait_ge(S["sq_ready"], PAIRS)
                        pe.matmul(bank[2][:, 0:T], ones[:, :], sqacc, start=True, stop=True
                                  ).then_inc(S["sq_psum"], 1)
                        pe.wait_ge(S["off_read"], PAIRS)
                    elif which == 3 and mm2 == 0:
                        pe.wait_ge(S["rs_ready"], 1)
                        pe.wait_ge(S["sf_ready"], PAIRS)
                        pe.wait_ge(S["y_ready"], PAIRS)
                    b = (0, 1, 1, 2, 3)[which]
                    i = n - FIRST_BRANCH
                    pe.wait_ge(S["branch_lo"], branch_split(("w", i)))
                    if c[0] == "bs":
                        pe.wait_ge(S["branch_lo"], branch_split(("y", 3)))
                    elif c[0] == "bm":
                        pe.wait_ge(S["branch_lo"], branch_split(("mlp", 0)))
                    w_h = wb_hi[:, i % 2, :].rearrange("p (k n) -> p k n", k=KD)
                    w_l = ring_r[:, n % RING, :].rearrange("p (k n) -> p k n", k=KD)
                    x_h, x_l, k0 = {"g": (hn_hi, hn_lo, 0), "s": (y_hi, y_lo, KD * (which - 1)),
                                    "m": (mlp_hi, mlp_lo, 0)}["g" if c[0][0] == "g" else c[0][1]]
                    for m in range(2):
                        for k in range(KD):
                            for w, v in ((w_h, x_h), (w_h, x_l), (w_l, x_h)):
                                mm = pe.matmul(bank[4 * m + b][:, 0:T], w[:, k, m * P:m * P + P], v[:, k0 + k, :],
                                               start=(k == 0 and which != 2 and v is x_h and w is w_h),
                                               stop=(k == KD - 1 and which != 1 and w is w_l))
                    mm.then_inc(chunk_used, 1)
            pe.wait_ge(S["merged"], 8)
            for m in range(4):
                chunk_ready(pe, ("out", m))
                w = pair_rows(AT[("out", m)] % RING)
                for c in range(3):
                    for k in range(2):
                        for half in range(2):
                            mm = pe.matmul(bank[2 * c + half][0:rows(c), :], mergedT[:, 2 * m + k, tok(c)],
                                           w[:, k, hb(c, half)], start=(m == 0 and k == 0),
                                           stop=(m == 3 and k == 1))
                    if m == 3 and c < 2:
                        mm.then_inc(S["out_psum"], 1)
                mm.then_inc(chunk_used, 1)

            pe.wait_ge(S["hf_ready"], 3)
            for k in range(KD):
                if k >= 2:
                    pe.wait_ge(S["hfT_ready"], k - 1)
                for c in range(3):
                    mm = turn(bank[6 + k % 2][:, tok(c)], hf[0:rows(c), c, k * P:k * P + P])
                mm.then_inc(S["hfT_psum"], 1)
            pe.wait_ge(S["hfT_ready"], KD)
            for c in range(3):
                for k in range(KD):
                    mm = pe.matmul(bank[0][0:rows(c), c * H:c * H + E], hfT[:, k, tok(c)], wr[:, k, :],
                                   start=(k == 0), stop=(k == KD - 1))
            mm.then_inc(S["lg_psum"], 1)
            pe.wait_ge(S["route_ready"], 3)
            for c in range(3):
                for i in range(c):
                    pe.matmul(bank[1][0:rows(c), c * H:c * H + E], ones[:, 0:rows(c)], chosen[:, i, :],
                              start=(i == 0), stop=False)
                mm = pe.matmul(bank[1][0:rows(c), c * H:c * H + E], before[0:rows(c), 0:rows(c)],
                               chosen[0:rows(c), c, :], start=(c == 0), stop=True)
            mm.then_inc(S["rank_psum"], 1)
            for c in range(3):
                mm = pe.matmul(bank[2][0:1, 0:E], ones[0:rows(c), 0:1], chosen[0:rows(c), c, :],
                               start=(c == 0), stop=(c == 2))
            mm.then_inc(S["cnt_psum"], 1)
            for c in range(3):
                mm = turn(bank[3][0:E, tok(c)], gates[0:rows(c), c, :])
            mm.then_inc(S["gT_psum"], 1)
            pe.wait_ge(S["gT_ready"], 1)
            pe.wait_ge(bd_in, 16)
            for n in range(6):
                c, half = n // 2, n % 2
                if n >= 2:
                    pe.wait_ge(S["bd_done"], n - 1)
                pe.matmul(bank[4 + n % 2][0:rows(c), :], gatesT[0:E, tok(c)], bd[0:E, hb(c, half)],
                          start=True, stop=True).then_inc(S["bd_psum"], 1)

            def dispatch(n, turned=None):
                pe.wait_ge(S["sel_ready"], n + 1)
                if isinstance(n, int) and n == 0:
                    pe.wait_ge(S["parts_hi"], 6)
                    pe.wait_ge(S["parts_rest"], 6)
                    pe.wait_ge(S["hfT_ready"], KD)
                if turned is not None:
                    pe.wait_ge(S["tk_ready"], turned)
                    pe.wait_ge(S["gate_ready"], turned)
                for k in range(KD):
                    for c in range(3):
                        for i in range(3):
                            mm = pe.matmul(bank[6 + k // 4][:, (k % 4) * P:(k % 4) * P + P],
                                           hfb[0:rows(c), i, c, k * P:k * P + P], take[0:rows(c), c, :],
                                           start=(c == 0 and i == 0), stop=(c == 2 and i == 2))
                mm.then_inc(S["xe_psum"], 1)

            def gate_up(n):
                pe.wait_ge(S["xe_ready"], n + 1)
                pe.wait_ge(S["xe_lo_ready"], n + 1)
                if isinstance(n, int) and n == 0:
                    pe.wait_ge(S["gT_ready"], 1)
                    pe.wait_ge(S["slot_ready"], 1)
                    pe.wait_ge(S["work_ready"], 1)
                else:
                    pe.wait_ge(S["at_lo_ready"], 2 * n)
                for j in range(7):
                    lo_made(pe, n, j)
                    b = j % SPLITS
                    for x, w in ((xe_hi, w_hi), (xe_hi, w_lo), (xe_lo, w_hi)):
                        for q in range(4):
                            mm = pe.matmul(bank[q][:, :], x[:, j, :], w[:, b, 512 * q:512 * q + 512],
                                           start=(j == 0 and x is xe_hi and w is w_hi), stop=False)
                    mm.then_inc(chunk_used, 1)
                lo_made(pe, n, 7)
                pe.wait_ge(S["bias_ready"], n + 1)
                for q in range(4):
                    cols = slice(512 * q, 512 * q + 512)
                    for x, w in ((xe_hi, w_hi), (xe_hi, w_lo), (xe_lo, w_hi)):
                        mm = pe.matmul(bank[q][:, :], x[:, 7, :], w[:, 7 % SPLITS, cols],
                                       start=False, stop=False)
                    if q == 3:
                        mm.then_inc(chunk_used, 1)
                    pe.matmul(bank[q][:, :], pick_bias[:, :], bgu_parts[:, cols],
                              start=False, stop=True).then_inc(S["gu_psum"], 1)

            def turn_act(n):
                for half in range(2):
                    pe.wait_ge(S["act_ready"], n * 4 + (2 * half + 2))
                    for f in range(4 * half, 4 * half + 4):
                        mm = turn(bank[half][:, (f % 4) * P:(f % 4) * P + P],
                                  lin[:, f // 2, (f % 2) * P:(f % 2) * P + P])
                    mm.then_inc(S["at_psum"], 1)

            def combine(n, pieces=range(6)):
                pe.wait_ge(S["ye_ready"], n + 1)
                pe.wait_ge(S["ye_lo_ready"], n + 1)
                for i in pieces:
                    c, half = i // 2, i % 2
                    if i >= 2:
                        pe.wait_ge(S["cm_done"], n * 6 + (i - 1))
                    for y in (ye_hi, ye_lo):
                        mm = pe.matmul(bank[2 + i % 2][:, :], takeT[:, P * c:P * c + P], y[:, hb(c, half)],
                                       start=(y is ye_hi), stop=(y is ye_lo))
                    mm.then_inc(S["cm_psum"], 1)

            def turn_take(n):
                pe.wait_ge(S["kept_ready"], n + 1)
                for c in range(3):
                    mm = pe.transpose(bank[6][:, :].bitcast(BF16)[:, tok(c)], kept[0:rows(c), c, :],
                                      ident_bf[0:rows(c), 0:rows(c)])
                mm.then_inc(S["tk_psum"], 1)
                for c in range(3):
                    mm = pe.matmul(bank[7][:, 0:3], kept[0:rows(c), c, :],
                                   gates3_of(n, c), start=(c == 0), stop=(c == 2))
                mm.then_inc(S["kept_used"], 1)

            expert = [None]

            def gates3_of(n, c):
                return gates3[0:rows(c), c, bass.ds(expert[0], 1), :].rearrange("p e i -> p (e i)")

            def down(n, e, pipelined=True, before_it=False):
                expert[0] = e
                for j in range(4):
                    if j == 0 and before_it:
                        combine(n - 1, (0, 1))
                    lo_made(pe, n, 8 + j)
                    b = (8 + j) % SPLITS
                    if j % 2 == 0:
                        pe.wait_ge(S["at_ready"], 2 * n + (j // 2 + 1))
                    if j == 0:
                        if isinstance(n, int) and n == 0:
                            pe.wait_ge(S["bd_done"], 6)
                        else:
                            pe.wait_ge(S["ye_lo_ready"], n)
                    for a, w in ((act_hi, w_hi), (act_hi, w_lo), (act_lo, w_hi)):
                        if a is act_lo and j % 2 == 0:
                            pe.wait_ge(S["at_lo_ready"], 2 * n + (j // 2 + 1))
                        for k in range(2):
                            for half in range(2):
                                mm = pe.matmul(bank[4 + half][:, :], a[:, 2 * j + k, :],
                                               w[:, b, D * k + 512 * half:D * k + 512 * half + 512],
                                               start=(j == 0 and k == 0 and a is act_hi and w is w_hi),
                                               stop=(j == 3 and k == 1 and a is act_lo))
                    mm.then_inc(chunk_used, 1)
                    if j < 2 and before_it:
                        combine(n - 1, (2 * j + 2, 2 * j + 3))
                    if j == 1:
                        if pipelined:
                            pe.wait_ge(S["xe_ready"], n + 2)
                            pe.wait_ge(S["xe_lo_ready"], n + 2)
                        turn_take(n)

            def block_of(n, first=False, last=False):
                gate_up(n)
                if not last:
                    dispatch(n + 1, None if first else n)
                turn_act(n)
                down(n, n, not last, not first)

            dispatch(0)
            block_of(0, first=True)
            with pe.Fori(1, E - 1) as n:
                block_of(n)
            block_of(E - 1, last=True)
            combine(E - 1)
            more = pe.value_load(work[0:1, 32:33], min_val=0, max_val=MAX_EXTRA)
            with pe.If(more > 0):
                with pe.Fori(0, more) as i:
                    n = i + E
                    e = pe.value_load(work[0:1, bass.ds(i, 1)], min_val=0, max_val=E - 1)
                    dispatch(n, n)
                    gate_up(n)
                    turn_act(n)
                    down(n, e, False)
                    combine(n)

        @block.scalar
        def _(act):
            link = chain(act, act_chain)

            def fn(out, in_, f, **kw):
                return act.activation(out, in_, f, **kw)

            act.wait_ge(x_in, 32)
            for c in range(3):
                fn(hnT.rearrange("p a b -> p (a b)")[0:rows(c), 0:D], hid[0:rows(c), c, :], ACT.Square,
                   accum_out=small[0:rows(c), 4 + c:5 + c]).then_inc(S["x_ss"], 1)
                act.wait_ge(S["x_ss"], c + 1)
            for c in range(3):
                act.wait_ge(S["x_var"], c + 1)
                act.sqrt(small[0:rows(c), 8 + c:9 + c], small[0:rows(c), 4 + c:5 + c]).then_inc(S["x_std"], 1)
            for k in range(KD):
                act.wait_ge(S["hnT_psum"], k + 1)
                act.copy(hnT[:, k, :], bank[k % 2][:, 0:T]).then_inc(S["hnT_ready"], 1)
            for m in range(8):
                act.wait_ge(S["proj_ready"], m + 1)
                if m >= 2:
                    act.wait_ge(S["vt_psum"], m - 1)
                fn(vT[:, m % 2, :], bank[m % 2][:, 0:T], ACT.Gelu).then_inc(S["proj_read"], 1)
                act.wait_ge(S["proj_read"], m + 1)
                act.sem_inc(S["vT_ready"], 1)
            for m in range(8):
                act.wait_ge(S["proj_ready"], 9 + m)
                fn(mlpT[:, m, :], bank[m % 2][:, 0:T], ACT.Gelu).then_inc(S["proj_read"], 1)
            for c in range(3):
                act.wait_ge(S["ln_var"], c + 1)
                act.sqrt(small[0:rows(c), 44 + c:45 + c], small[0:rows(c), 40 + c:41 + c]).then_inc(S["ln_std"], 1)
            act.wait_ge(S["dt_abs"], 1)
            fn(dtmp[0:H, 3, :], dtmp[0:H, 2, :], ACT.Exp)
            fn(small[0:H, 2:3], small[0:H, 1:2], ACT.Exp).then_inc(S["dt_exp"], 1)
            act.wait_ge(S["dt_u"], 1)
            fn(dtmp[0:H, 5, :], dtmp[0:H, 4, :], ACT.Ln).then_inc(S["dt_ln"], 1)
            act.wait_ge(S["acum_ready"], 1)
            fn(dtmp[0:H, 3, :], dtmp[0:H, 2, :], ACT.Exp)
            fn(small[0:H, 3:4], acumT[0:H, SEQ - 1:SEQ], ACT.Exp)
            fn(eacT[0:H, :], acumT[0:H, :], ACT.Exp).then_inc(S["dt_exp"], 1)
            act.wait_ge(S["v_ready"], 3)
            act.dma_start(v_sample_new[0].rearrange("b l d -> (b l) d"), vtok[0:NS, 2, :]).then_inc(v_out, 16)
            act.wait_ge(S["mix_read"], GH)
            act.wait_ge(v_out, 16)
            act.wait_ge(S["pre_ready"], 2)
            for j in range(2):
                act.dma_start(s_in[j], state_ssm[0].rearrange("b h p n -> (h p) b n")[P * j:P * j + P]
                              ).then_inc(s_in_full[j], 16)

            def conv_group(g):
                q = Q_DT + 1 + 10 * g
                if g >= 2:
                    act.wait_ge(S["yd_psum"], 4 * g - 4)
                    act.wait_ge(S["y_ready"], 4 * g - 4)

                def silu(t):
                    n = g * CG + t
                    act.wait_ge(S["conv_done"], n + 1)
                    dst = xsT[g % 2][:, t, :] if t < 4 else bcT[g % 2][:, t - 4, :]
                    fn(dst, acc[:, n % 2, :], ACT.Silu).then_inc(S["conv_act"], 1)

                for t in range(CG):
                    n = g * CG + t
                    b = bank[(q + t) % 2]
                    ch = xchan(g, t)
                    act.wait_ge(S["proj_ready"], q + t + 1)
                    if n >= 2:
                        act.wait_ge(S["conv_done"], n - 1)
                        act.wait_ge(S["packed"], n - 1)
                        act.wait_ge(S["conv_act"], n - 1)
                    act.copy(raw[:, n % 2, KEEP:SPAN], b[:, 0:SEQ])
                    act.copy(raw[:, n % 2, SPAN:].rearrange("p (b k) -> p b k", k=STEP)[:, :, KEEP:],
                             b[:, SEQ:T].rearrange("p (b k) -> p b k", k=DS)).then_inc(S["raw_ready"], 1)
                    fn(acc[:, n % 2, :], b[:, 0:T], ACT.Identity, scale=convv[:, 72 + ch:73 + ch],
                       bias=convv[:, 96 + ch:97 + ch]).then_inc(S["proj_read"], 1)
                    if t:
                        silu(t - 1)
                silu(CG - 1)
                for t in range(4):
                    act.wait_ge(S["proj_ready"], q + CG + t + 1)
                    fn(yT[:, 4 * g + t, :], bank[(q + CG + t) % 2][:, 0:T], ACT.Silu).then_inc(S["proj_read"], 1)
                act.wait_ge(S["cs_psum"], g + 1)
                act.copy(csout[0:STATE_ROWS, 512 * g:512 * g + 512], bank[2][0:STATE_ROWS, :])
                act.copy(csout[0:STATE_ROWS, DI + N * g:DI + N * g + N], bank[4][0:STATE_ROWS, 0:P])
                act.copy(csout[0:STATE_ROWS, DI + (G + g) * N:DI + (G + g) * N + N], bank[4][0:STATE_ROWS, P:2 * P]
                         ).then_inc(S["cs_ready"], 1)

            def ssd_group(g):
                act.wait_ge(S["bt_psum"], g + 1)
                if g:
                    act.wait_ge(S["bm_ready"], g)
                act.copy(btok[:, 0:2, :], bank[6][:, 0:2 * P].rearrange("p (c n) -> p c n", c=2))
                for i in range(2):
                    act.copy(b_hi[i * NS:i * NS + NS, :], bank[6][0:NS, 2 * P:3 * P])
                act.copy(btok[0:NS, 2, :], bank[6][0:NS, 2 * P:3 * P]).then_inc(S["bt_ready"], 1)
                for j in range(4 * g, 4 * g + 4):
                    p = j % 2
                    act.wait_ge(S["e_psum"], j + 1)
                    if j >= 2:
                        act.wait_ge(S["sn_ready"], j - 1)
                        act.wait_ge(S["off_read"], j - 1)
                    for hh in range(2):
                        rows_of = slice(HP * hh, HP * hh + HP)
                        i = act.copy(esb[rows_of, p, :], bank[5][rows_of, (T - P) * hh:(T - P) * hh + T - P])
                    i.then_inc(S["e_ready"], 1)
                    act.wait_ge(S["sT_psum"], j + 1)
                    if j >= 2:
                        act.wait_ge(S["off_psum"], j - 1)
                    for half in range(2):
                        act.copy(s_T[p][:, 4 * half:4 * half + 4, :],
                                 bank[half][:, :].rearrange("p (b n) -> p b n", b=4)).then_inc(S["sT_ready"], 1)
                    act.wait_ge(S["sf_psum"], j + 1)
                    act.copy(s_0T[:, p, :], bank[6][:, 0:P]).then_inc(S["s0_ready"], 1)
                    if j >= 2:
                        act.wait_ge(s_fin_out[p], 16 * (j // 2))
                    act.copy(s_fin[:, p, :], bank[6][:, P:2 * P]).then_inc(S["sf_ready"], 1)
                    act.wait_ge(S["seg_ready"], j + 1)
                    if j:
                        act.wait_ge(S["yd_psum"], j)
                    fn(dec, seg, ACT.Exp).then_inc(S["exp_ready"], 1)
                    act.wait_ge(S["sf_ready"], j + 1)
                    act.dma_start(ssm_prompt_new[0, 0].rearrange("h p n -> (h p) n")[P * j:P * j + P],
                                  s_fin[:, p, :]).then_inc(s_fin_out[p], 16)
                    act.wait_ge(S["sn_ready"], j + 1)
                    act.dma_start(ssm_sample_new[0].rearrange("b h p n -> (h p) b n")[P * j:P * j + P],
                                  s_new).then_inc(s_new_out, 16)
                    if j + 2 < PAIRS:
                        act.dma_start(s_in[p], state_ssm[0].rearrange("b h p n -> (h p) b n")[P * (j + 2):P * (j + 3)]
                                      ).then_inc(s_in_full[p], 16)

            for step in range(G + 1):
                if step < G:
                    conv_group(step)
                if step:
                    ssd_group(step - 1)
            act.wait_ge(cs_out, 32)
            act.wait_ge(S["y_ready"], PAIRS)
            act.wait_ge(S["yd_psum"], PAIRS)

            def gates_of(which, q):
                act.wait_ge(chunk_used, AT[(which, q)] - N_PROJ + 1)
                if q and which == "gs":
                    act.wait_ge(S["merged"], 2 * q)
                for m in range(2):
                    i = fn((gate_s if which == "gs" else gate_m)[:, m, :],
                           bank[4 * m + (0 if which == "gs" else 2)][:, 0:T], ACT.Sigmoid)
                    if which == "gm":
                        i.then_inc(S["gates_ready"], 1)

            for item in BRANCH:
                kind, i = item
                v, hi, _ = branch_item(item)
                if kind == "w":
                    c = CHUNKS[FIRST_BRANCH + i]
                    chunk_ready(act, c)
                    if i >= 2:
                        act.wait_ge(chunk_used, FIRST_BRANCH + i - 2 - N_PROJ + 1)
                if kind == "y":
                    act.wait_ge(s_new_out, 16 * PAIRS)
                    act.wait_ge(s_fin_out[0], 16 * PAIRS // 2)
                    act.wait_ge(s_fin_out[1], 16 * PAIRS // 2)
                    act.wait_ge(S["sq_ready"], 4 * i + 4)
                act.copy(hi, v).then_inc(S["branch_hi"], 1)
                if item == ("w", 1):
                    act.wait_ge(S["rs_var"], 1)
                    act.sqrt(rstd_row, rstd_row).then_inc(S["rs_std"], 1)
                if kind == "w" and i % 5 == 2:
                    gates_of("gs", i // 5)
                if kind == "w" and i % 5 == 0 and i:
                    gates_of("gm", i // 5 - 1)
            gates_of("gm", 3)
            act.wait_ge(s_fin_out[0], 16 * PAIRS // 2)
            act.wait_ge(s_fin_out[1], 16 * PAIRS // 2)
            act.wait_ge(s_new_out, 16 * PAIRS)
            for c in range(3):
                act.wait_ge(S["h_ready"], c + 1)
                fn(hf_rest[0:rows(c), c, :], hid[0:rows(c), c, :], ACT.Square,
                   accum_out=small[0:rows(c), 16 + c:17 + c]).then_inc(S["h_ss"], 1)
                act.wait_ge(S["h_var"], c + 1)
                act.sqrt(small[0:rows(c), 20 + c:21 + c], small[0:rows(c), 16 + c:17 + c]).then_inc(S["h_std"], 1)
            for c in range(3):
                act.wait_ge(S["hf_ready"], c + 1)
                act.copy(hfb[0:rows(c), 0, c, :], hf[0:rows(c), c, :]).then_inc(S["parts_hi"], 1)
            for k in range(KD):
                act.wait_ge(S["hfT_psum"], k + 1)
                act.copy(hfT[:, k, :], bank[6 + k % 2][:, 0:T]).then_inc(S["hfT_ready"], 1)
            for c in range(3):
                act.wait_ge(S["parts_rest"], c + 1)
                act.copy(hfb[0:rows(c), 1, c, :], hf_rest[0:rows(c), c, :]).then_inc(S["parts_hi"], 1)
            for c in range(3):
                act.wait_ge(S["lg_ready"], c + 1)
                fn(expd[0:rows(c), c, :], logits[0:rows(c), c, 0:E], ACT.Exp,
                   bias=small[0:rows(c), 24 + c:25 + c]).then_inc(S["ge_ready"], 1)
            act.wait_ge(S["gT_psum"], 1)
            act.copy(gatesT[0:E, :], bank[3][0:E, 0:T]).then_inc(S["gT_ready"], 1)

            def split_hi(n, j):
                expert_slot_ready(act, n, j)
                if isinstance(n, int) and n == 0 and j < SPLITS:
                    act.wait_ge(S["early_done"], 1)
                else:
                    act.wait_ge(chunk_used, n * EXPERT_CHUNKS + (USED_MIXER + j - SPLITS + 1))
                act.copy(w_hi[:, j % SPLITS, :], ring[:, slot_of(j), :]).then_inc(S["hi_ready"], 1)

            def read_inputs(n):
                act.wait_ge(S["xe_psum"], n + 1)
                for half in range(2):
                    i = act.copy(xe_hi[:, 4 * half:4 * half + 4, :],
                                 bank[6 + half][:, :].rearrange("p (k t) -> p k t", k=4))
                i.then_inc(S["xe_ready"], 1)

            def sigmoids(n):
                for q in range(4):
                    act.wait_ge(S["glu_ready"], n * 4 + (q + 1))
                    fn(sig[:, q, :], glu[:, q, :], ACT.Sigmoid, scale=ALPHA).then_inc(S["sig_ready"], 1)

            def read_act(n):
                for half in range(2):
                    act.wait_ge(S["at_psum"], 2 * n + (half + 1))
                    act.copy(act_hi[:, 4 * half:4 * half + 4, :],
                             bank[half][:, :].rearrange("p (k t) -> p k t", k=4)).then_inc(S["at_ready"], 1)

            def read_take(n):
                act.wait_ge(S["tk_psum"], n + 1)
                act.copy(takeT[:, 0:T], bank[6][:, :].bitcast(BF16)[:, 0:T]).then_inc(S["tk_ready"], 1)

            def read_out(n):
                act.wait_ge(chunk_used, n * EXPERT_CHUNKS + (USED_MIXER + EXPERT_CHUNKS))
                act.wait_ge(S["gate_ready"], n + 1)
                for half in range(2):
                    i = act.mul(ye_hi[:, hb(0, half)], bank[4 + half][:, :], gate_of[:, 0:1])
                i.then_inc(S["ye_ready"], 1)

            def block_of(n, last=False):
                for j in range(LEAD, 7 + LEAD):
                    split_hi(n, j)
                sigmoids(n)
                split_hi(n, 7 + LEAD)
                read_act(n)
                if not last:
                    read_inputs(n + 1)
                for j in range(8 + LEAD, EXPERT_CHUNKS):
                    split_hi(n, j)
                read_take(n)
                if not last:
                    for j in range(LEAD):
                        split_hi(n + 1, j)
                read_out(n)

            for j in range(LEAD):
                split_hi(0, j)
            read_inputs(0)
            block_of(0)
            with act.Fori(1, E - 1) as n:
                block_of(n)
            block_of(E - 1, last=True)
            act.wait_ge(S["work_ready"], 1)
            more = act.value_load(work[0:1, 32:33], min_val=0, max_val=MAX_EXTRA)
            with act.If(more > 0):
                with act.Fori(0, more) as i:
                    n = i + E
                    for j in range(LEAD):
                        split_hi(n, j)
                    read_inputs(n)
                    block_of(n, last=True)
            for c in range(3):
                act.wait_ge(S["all_added"], 1)
                fn(junk2[0:rows(c)], hid[0:rows(c), c, :], ACT.Square,
                   accum_out=small[0:rows(c), 28 + c:29 + c]).then_inc(S["y_ss"], 1)
                act.wait_ge(S["y_ss"], c + 1)
            for c in range(3):
                act.wait_ge(S["y_var"], c + 1)
                act.sqrt(small[0:rows(c), 32 + c:33 + c], small[0:rows(c), 28 + c:29 + c]).then_inc(S["y_std"], 1)
            act.wait_ge(S["y_out"], 3)
            act.dma_start(y_prompt[0].rearrange("(c p) d -> p c d", p=P), hid[:, 0:2, :]).then_inc(stored, 16)
            act.dma_start(y_sample.rearrange("b l d -> (b l) d"), hid[0:NS, 2, :]).then_inc(stored, 16)
            act.wait_ge(stored, 32)
            act.wait_ge(s_fin_out[0], 16 * PAIRS // 2)
            act.wait_ge(s_fin_out[1], 16 * PAIRS // 2)
            act.wait_ge(s_new_out, 16 * PAIRS)
            act.wait_ge(cs_out, 32)

        @block.vector
        def _(dve):
            link = chain(dve, dve_chain)

            def var(dst, n, count):
                return dve.tensor_scalar(dst, dst, 1.0 / count, EPS, ALU.mult, ALU.add)

            for c in range(3):
                dve.wait_ge(S["x_ss"], c + 1)
                var(small[0:rows(c), 4 + c:5 + c], c, D).then_inc(S["x_var"], 1)
            dve.wait_ge(rows_in, 16)
            for c in range(3):
                dve.wait_ge(S["x_std"], c + 1)
                link(dve.reciprocal(small[0:rows(c), 12 + c:13 + c], small[0:rows(c), 8 + c:9 + c]))
                dve.scalar_tensor_tensor(hn[0:rows(c), c, :], hid[0:rows(c), c, :], small[0:rows(c), 12 + c:13 + c],
                                         nm_row[0:rows(c)], ALU.mult, ALU.mult).then_inc(S["hn_ready"], 1)
            dve.wait_ge(S["vec_psum"], 1)
            dve.tensor_copy(convv[:], bank[2][:, 0:120])
            dve.tensor_copy(gn_col[:], bank[2][:, 120:120 + PAIRS]).then_inc(S["vec_ready"], 1)
            for half in range(2):
                dve.wait_ge(S["pre_psum"], half + 1)
                dve.tensor_copy(prefix[:, half * 12:half * 12 + 12, :],
                                bank[3 + half][:, 0:288].rearrange("p (a b) -> p a b", a=12)
                                ).then_inc(S["pre_ready"], 1)
            dve.wait_ge(S["ws_psum"], 1)
            dve.wait_ge(consts, 1)
            for half in range(2):
                i = dve.tensor_tensor(wsT[:, 4 * half:4 * half + 4, :],
                                      bank[5 + half][:, :].rearrange("p (g t) -> p g t", g=4),
                                      causal[:, 0:P].unsqueeze(1).to_broadcast([P, 4, P]), ALU.mult)
            i.then_inc(S["ws_ready"], 1)
            dve.wait_ge(S["ws_psum"], 2)
            dve.tensor_tensor(wsS[0:NS].rearrange("p g (b l) -> p g b l", b=DB),
                              bank[7][0:NS, 0:GH * DS].rearrange("p (g l) -> p g l", g=GH).unsqueeze(2)
                              .to_broadcast([NS, GH, DB, DS]),
                              samebatch[0:NS].unsqueeze(1).unsqueeze(3).to_broadcast([NS, GH, DB, DS]), ALU.mult
                              ).then_inc(S["ws_ready"], 1)
            for m in range(8):
                dve.wait_ge(S["vt_psum"], m + 1)
                b = bank[2 + m % 2]
                dve.tensor_copy(vtok[:, 0:2, m * P:m * P + P], b[:, 0:2 * P].rearrange("p (c n) -> p c n", c=2))
                dve.tensor_copy(vtok[0:NS, 2, m * P:m * P + P], b[0:NS, 2 * P:3 * P]).then_inc(S["vt_ready"], 1)
            dve.wait_ge(S["vt_ready"], 8)
            dve.wait_ge(heads_in, 96)
            stats = ring_stats = small[:, 48:60]
            for c in range(3):
                r = rows(c)
                for half in range(2):
                    i = dve.bn_stats(small[0:r, 48 + 6 * half:54 + 6 * half], vtok[0:r, c, hb(c, half)])
                link(i)
                link(dve.bn_aggr(small[0:r, 34 + 2 * c:36 + 2 * c], small[0:r, 48:60]))
                dve.tensor_scalar(small[0:r, 40 + c:41 + c], small[0:r, 35 + 2 * c:36 + 2 * c], EPS, None, ALU.add
                                  ).then_inc(S["ln_var"], 1)
            for c in range(3):
                r = rows(c)
                dve.wait_ge(S["ln_std"], c + 1)
                link(dve.reciprocal(small[0:r, 60 + c:61 + c], small[0:r, 44 + c:45 + c]))
                link(dve.tensor_scalar(vtok[0:r, c, :], vtok[0:r, c, :], small[0:r, 34 + 2 * c:35 + 2 * c],
                                       small[0:r, 60 + c:61 + c], ALU.subtract, ALU.mult))
                link(dve.tensor_tensor(vtok[0:r, c, :], vtok[0:r, c, :], vw_row[0:r], ALU.mult))
                dve.tensor_tensor(vtok[0:r, c, :], vtok[0:r, c, :], vb_row[0:r], ALU.add
                                  ).then_inc(S["v_ready"], 1)
            dve.wait_ge(S["proj_ready"], Q_DT + 1)
            x, m, u, rest = dtmp[0:H, 0, :], dtmp[0:H, 1, :], dtmp[0:H, 4, :], dtmp[0:H, 6, :]
            dve.tensor_scalar(x, bank[Q_DT % 2][0:H, 0:T], small[0:H, 0:1], None, ALU.add
                              ).then_inc(S["proj_read"], 1)
            dve.wait_ge(S["proj_read"], Q_DT + 1)
            dve.scalar_tensor_tensor(dtmp[0:H, 2, :], x, -1.0, x, ALU.mult, ALU.min).then_inc(S["dt_abs"], 1)
            link(dve.tensor_scalar(m, x, 0.0, None, ALU.max))
            dve.wait_ge(S["dt_exp"], 1)
            dve.tensor_scalar(u, dtmp[0:H, 3, :], 1.0, None, ALU.add).then_inc(S["dt_u"], 1)
            dve.wait_ge(S["dt_u"], 1)
            link(dve.tensor_scalar(rest, u, -1.0, None, ALU.add))
            link(dve.tensor_tensor(rest, dtmp[0:H, 3, :], rest, ALU.subtract))
            link(dve.reciprocal(dtmp[0:H, 7, :], u))
            link(dve.tensor_tensor(rest, rest, dtmp[0:H, 7, :], ALU.mult))
            link(dve.tensor_tensor(rest, rest, m, ALU.add))
            dve.wait_ge(S["dt_ln"], 1)
            link(dve.tensor_tensor(x, dtmp[0:H, 5, :], rest, ALU.add))
            link(dve.tensor_scalar(m, x, small[0:H, 2:3], -1.0, ALU.mult, ALU.mult))
            link(dve.tensor_tensor_scan(acumT[0:H, :], running[:], m, 0.0, ALU.mult, ALU.add))
            for c in range(2):
                e = TILES[c][0] + P - 1
                dve.tensor_scalar(dtmp[0:H, 2, tok(c)], acumT[0:H, tok(c)], -1.0, acumT[0:H, e:e + 1],
                                  ALU.mult, ALU.add)
            dve.tensor_tensor(dtmp[0:H, 2, SEQ:T].rearrange("p (b l) -> p b l", b=DB),
                              acumT[0:H, SEQ + DS - 1:T:DS].unsqueeze(2).to_broadcast([H, DB, DS]),
                              acumT[0:H, SEQ:T].rearrange("p (b l) -> p b l", b=DB), ALU.subtract
                              ).then_inc(S["acum_ready"], 1)
            dve.wait_ge(S["dt_exp"], 2)
            for i, v in enumerate((acumT, eacT)):
                link(dve.tensor_copy(head_parts[0:H, i, :], v[0:H, :]))
                link(dve.tensor_tensor(head_parts[H:2 * H, i, :], v[0:H, :], head_parts[0:H, i, :].bitcast(F32),
                                       ALU.subtract))
            link(dve.tensor_tensor(dtmp[0:H, 3, :], dtmp[0:H, 3, :], x, ALU.mult))
            dve.tensor_scalar(dtmp[0:H, 4, 0:P], dtmp[0:H, 3, 0:P], small[0:H, 3:4], None, ALU.mult
                              ).then_inc(S["dt_w"], 1)
            for g in range(GH):
                dve.wait_ge(S["mix_psum"], g + 1)
                dve.wait_ge(S["proj_read"], 16)
                dve.tensor_tensor(mlpT[:, g, :], mlpT[:, g, :], bank[4 + g % 2][:, 0:T], ALU.mult
                                  ).then_inc(S["mix_read"], 1)
            link(dve.memset(tm[:, :, :], 0.0))
            dve.wait_ge(S["tm_psum"], 1)
            dve.tensor_copy(tm[:, 0:3, 0:2 * H],
                            bank[2][:, 0:288].rearrange("p (a b) -> p a b", a=3)[:, :, 0:2 * H])
            dve.tensor_copy(tm[0:NS, 0:3, 2 * H:3 * H],
                            bank[2][0:NS, 0:288].rearrange("p (a b) -> p a b", a=3)[:, :, 2 * H:3 * H])
            link(dve.tensor_copy(tm[:, 3, 0:H], bank[2][:, 288:288 + H]))
            dve.sem_inc(S["tm_ready"], 1)

            def conv_group(g):
                for t in range(CG):
                    n = g * CG + t
                    ch = xchan(g, t)
                    dve.wait_ge(S["raw_ready"], n + 1)
                    dve.wait_ge(S["pre_copied"], n + 1)
                    dve.wait_ge(S["proj_read"], Q_DT + 2 + 10 * g + t)
                    a = acc[:, n % 2, :]
                    r = raw[:, n % 2, SPAN:].rearrange("p (b k) -> p b k", k=STEP)
                    for k in range(TAPS - 1):
                        w = convv[:, CT * k + ch:CT * k + ch + 1]
                        dve.scalar_tensor_tensor(a[:, 0:SEQ], raw[:, n % 2, k:k + SEQ], w, a[:, 0:SEQ],
                                                 ALU.mult, ALU.add)
                        i = dve.scalar_tensor_tensor(a[:, SEQ:T].rearrange("p (b k) -> p b k", k=DS),
                                                     r[:, :, k:k + DS], w,
                                                     a[:, SEQ:T].rearrange("p (b k) -> p b k", k=DS),
                                                     ALU.mult, ALU.add)
                        if k < TAPS - 2:
                            link(i)
                        else:
                            i.then_inc(S["conv_done"], 1)

            def ssd_group(g):
                dve.wait_ge(S["cb_psum"], g + 1)
                if g:
                    dve.wait_ge(S["decay_ready"], 4 * g)
                dve.tensor_tensor(cbm[:, 0:SEQ], bank[7][:, 0:SEQ], causal[:, 0:SEQ], ALU.mult)
                dve.tensor_tensor(cbm[0:NS, SEQ:T], bank[7][0:NS, SEQ:T], causal[0:NS, SEQ:T], ALU.mult
                                  ).then_inc(S["cb_ready"], 1)
                def weigh(j):
                    p = j % 2

                    def heads(out, kind, c0, c1, r):
                        f = tm[0:r, kind, c0 * H:c1 * H].rearrange("p (c h) -> p c h", h=H)[:, :, 2 * j:2 * j + 2]
                        return dve.tensor_tensor(
                            out[0:r, c0 * P:c1 * P].rearrange("p (c h d) -> p c h d", h=2, d=HP),
                            bank[2][0:r, c0 * P:c1 * P].rearrange("p (c h d) -> p c h d", h=2, d=HP),
                            f.unsqueeze(3).to_broadcast([r, c1 - c0, 2, HP]), ALU.mult)

                    dve.wait_ge(S["xt_psum"], j + 1)
                    if j >= 2:
                        dve.wait_ge(S["yd_psum"], j - 1)
                    heads(xdt[:, p, :], 0, 0, 2, P)
                    heads(xdt[:, p, :], 0, 2, 3, NS)
                    heads(xw[:, p, :], 2, 0, 2, P)
                    heads(xw[:, p, :], 2, 2, 3, NS)
                    heads(xf[:, p, :], 3, 0, 1, P).then_inc(S["xw_ready"], 1)
                    dve.wait_ge(S["xw_ready"], j + 1)
                    dve.tensor_copy(xs[0:NS, p, :], xw[0:NS, p, 2 * P:3 * P]).then_inc(S["xs_hi"], 1)
                    dve.wait_ge(S["xs_hi"], j + 1)
                    dve.tensor_tensor(xs[NS:2 * NS, p, :], xw[0:NS, p, 2 * P:3 * P], xs[0:NS, p, :].bitcast(F32),
                                      ALU.subtract).then_inc(S["xs_ready"], 1)

                weigh(4 * g)
                for j in range(4 * g, 4 * g + 4):
                    p = j % 2
                    jj = j - 4 * g
                    dve.wait_ge(S["head_psum"], j + 1)
                    if j:
                        dve.wait_ge(S["exp_ready"], j)
                    for hh in range(2):
                        for c in range(3):
                            h = c * H + 2 * j + hh
                            i = dve.tensor_scalar(seg[:, hh, tok(c)], bank[3 + hh][:, tok(c)], tm[:, 1, h:h + 1],
                                                  0.0, ALU.subtract, ALU.min)
                    i.then_inc(S["seg_ready"], 1)
                    dve.wait_ge(S["sn_psum"], j + 1)
                    dve.wait_ge(S["e_ready"], j + 1)
                    if j:
                        dve.wait_ge(s_new_out, 16 * j)
                    for b in range(DB):
                        i = dve.scalar_tensor_tensor(
                            s_new[:, b, :], s_in[p][:, b, :], esb[:, p, P + DS * b + DS - 1:P + DS * b + DS],
                            bank[b // 4][:, (b % 4) * P:(b % 4) * P + P], ALU.mult, ALU.add)
                    i.then_inc(S["sn_ready"], 1)
                    dve.wait_ge(S["off_psum"], j + 1)
                    dve.tensor_tensor(off, bank[5][:, T - P:2 * T - 2 * P], esb[:, p, :], ALU.mult
                                      ).then_inc(S["off_read"], 1)
                    if jj < 3:
                        weigh(j + 1)
                    dve.wait_ge(S["yd_psum"], j + 1)
                    dve.wait_ge(heads_in, 96)
                    link(dve.scalar_tensor_tensor(ysum, xsT[g % 2][:, jj, :], ds_col[:, j:j + 1],
                                                  bank[7][:, 0:T], ALU.mult, ALU.add))
                    link(dve.tensor_tensor(ysum[:, P:T], ysum[:, P:T], off, ALU.add))
                    dve.wait_ge(S["proj_read"], Q_DT + 1 + 10 * g + 10)
                    dve.tensor_tensor(yT[:, j, :], yT[:, j, :], ysum, ALU.mult).then_inc(S["y_ready"], 1)

            for step in range(G + 1):
                if step < G:
                    conv_group(step)
                if step:
                    ssd_group(step - 1)

            dve.wait_ge(cs_out, 32)

            def merge(q):
                dve.wait_ge(chunk_used, AT[("bm", q)] - N_PROJ + 1)
                for m in (2 * q, 2 * q + 1):
                    b = 4 * (m % 2)
                    dve.wait_ge(S["gates_ready"], m + 1)
                    dve.tensor_tensor(part_s[:, m % 2, :], gate_s[:, m % 2, :], bank[b + 1][:, 0:T], ALU.mult)
                    link(dve.tensor_tensor(part_m[:, m % 2, :], gate_m[:, m % 2, :], bank[b + 3][:, 0:T], ALU.mult))
                    link(dve.tensor_tensor(part_s[:, m % 2, :], part_s[:, m % 2, :], rstd_row, ALU.mult))
                    dve.tensor_tensor(mergedT[:, m, :], part_s[:, m % 2, :], part_m[:, m % 2, :], ALU.add
                                      ).then_inc(S["merged"], 1)

            for item in BRANCH:
                kind, i = item
                v, hi, lo = branch_item(item)
                if kind == "w" and i % 5 == 1 and i > 5:
                    merge(i // 5 - 1)
                dve.wait_ge(S["branch_hi"], branch_split(item))
                dve.tensor_tensor(lo, v, hi.bitcast(F32), ALU.subtract).then_inc(S["branch_lo"], 1)
                if item == ("w", 1):
                    dve.wait_ge(S["sq_psum"], 1)
                    dve.tensor_scalar(rstd_row, bank[2][:, 0:T], 1.0 / DI, EPS, ALU.mult, ALU.add
                                      ).then_inc(S["rs_var"], 1)
                    dve.wait_ge(S["rs_std"], 1)
                    dve.reciprocal(rstd_row, rstd_row).then_inc(S["rs_ready"], 1)
                    dve.wait_ge(S["rs_ready"], 1)
            merge(3)
            for c in range(3):
                if c < 2:
                    dve.wait_ge(S["out_psum"], c + 1)
                else:
                    dve.wait_ge(chunk_used, USED_MIXER)
                for half in range(2):
                    i = dve.tensor_tensor(hid[0:rows(c), c, hb(c, half)], hid[0:rows(c), c, hb(c, half)],
                                          bank[2 * c + half][0:rows(c), :], ALU.add)
                i.then_inc(S["h_ready"], 1)
            for c in range(3):
                dve.wait_ge(S["h_ss"], c + 1)
                var(small[0:rows(c), 16 + c:17 + c], c, D).then_inc(S["h_var"], 1)
            dve.wait_ge(moe_in, 80)
            dve.wait_ge(S["bgu_ready"], 1)
            dve.wait_ge(s_fin_out[0], 16 * PAIRS // 2)
            dve.wait_ge(s_fin_out[1], 16 * PAIRS // 2)
            for c in range(3):
                dve.wait_ge(S["h_std"], c + 1)
                link(dve.reciprocal(small[0:rows(c), 12 + c:13 + c], small[0:rows(c), 20 + c:21 + c]))
                dve.scalar_tensor_tensor(hf[0:rows(c), c, :], hid[0:rows(c), c, :], small[0:rows(c), 12 + c:13 + c],
                                         nf_row[0:rows(c)], ALU.mult, ALU.mult).then_inc(S["hf_ready"], 1)
            for i in range(2):
                for c in range(3):
                    r = rows(c)
                    dve.wait_ge(S["parts_hi"], 3 * i + c + 1)
                    dst = hf_rest[0:r, c, :] if i == 0 else hfb[0:r, 2, c, :]
                    dve.tensor_tensor(dst, (hf if i == 0 else hf_rest)[0:r, c, :], hfb[0:r, i, c, :],
                                      ALU.subtract).then_inc(S["parts_rest"], 1)
            BIG = 3.0e38
            dve.wait_ge(S["lg_psum"], 1)
            link(dve.memset(logits[:, :, E:E + 4], BIG))
            link(dve.memset(gates[:, 2, :], 0.0))
            for c in range(3):
                r = rows(c)
                link(dve.tensor_tensor(logits[0:r, c, 0:E], bank[0][0:r, c * H:c * H + E], br_row[0:r], ALU.add))
                link(dve.max(best[0:r, c, :], logits[0:r, c, 0:E]))
                link(dve.tensor_scalar(small[0:r, 24 + c:25 + c], best[0:r, c, 0:1], -1.0, None, ALU.mult))
                link(dve.memset(best[0:r, c, 4:8], BIG))
                dve.sem_inc(S["lg_ready"], 1)
                link(dve.match_replace(swept[0:r, c, :], best[0:r, c, :], logits[0:r, c, :], -BIG))
                link(dve.tensor_tensor(chosen[0:r, c, :], swept[0:r, c, 0:E], logits[0:r, c, 0:E], ALU.not_equal))
                dve.wait_ge(S["ge_ready"], c + 1)
                link(dve.scalar_tensor_tensor(gates[0:r, c, :], expd[0:r, c, :], 1.0, chosen[0:r, c, :],
                                              ALU.mult, ALU.mult))
                link(dve.reduce_sum(small[0:r, 50 + c:51 + c], gates[0:r, c, :], AX.X))
                link(dve.reciprocal(small[0:r, 54 + c:55 + c], small[0:r, 50 + c:51 + c]))
                link(dve.tensor_scalar(gates[0:r, c, :], gates[0:r, c, :], small[0:r, 54 + c:55 + c], None,
                                       ALU.mult))
                dve.sem_inc(S["route_ready"], 1)
            dve.wait_ge(S["rank_psum"], 1)
            for c in range(3):
                r = rows(c)
                link(dve.scalar_tensor_tensor(slot_no[0:r, c, :], bank[1][0:r, c * H:c * H + E], 1.0,
                                              chosen[0:r, c, :], ALU.add, ALU.mult))
                link(dve.tensor_scalar(slot_no[0:r, c, :], slot_no[0:r, c, :], -1.0, None, ALU.add))
            dve.sem_inc(S["slot_ready"], 1)

            def select(n, e, first):
                if not isinstance(n, int) or n:
                    dve.wait_ge(S["xe_psum"], n)
                    dve.wait_ge(S["kept_ready"], n)
                for c in range(3):
                    r = rows(c)
                    i = dve.tensor_scalar(take[0:r, c, :], slots[0:r, bass.ds(first, P)],
                                          slot_no[0:r, c, bass.ds(e, 1)], None, ALU.is_equal)
                i.then_inc(S["sel_ready"], 1)

            def pick(n, e):
                if not isinstance(n, int) or n:
                    dve.wait_ge(S["gu_psum"], n * 4)
                dve.tensor_scalar(pick_bias[:, :], row_expert[:, :], slots[0:96, bass.ds(e, 1)], None,
                                  ALU.is_equal).then_inc(S["bias_ready"], 1)

            def split_lo(n, j):
                if j in ON_POOL:
                    return
                dve.wait_ge(S["hi_ready"], n * EXPERT_CHUNKS + (j + 1))
                dve.tensor_tensor(w_lo[:, j % SPLITS, :], ring[:, slot_of(j), :],
                                  w_hi[:, j % SPLITS, :].bitcast(F32), ALU.subtract).then_inc(S["lo_dve"], 1)

            def rest(out, hi, psum, half):
                s4 = slice(4 * half, 4 * half + 4)
                return dve.tensor_tensor(out[:, s4, :], bank[psum + half][:, :].rearrange("p (k t) -> p k t", k=4),
                                         hi[:, s4, :].bitcast(F32), ALU.subtract)

            def inputs_lo(n):
                dve.wait_ge(S["xe_ready"], n + 1)
                for half in range(2):
                    i = rest(xe_lo, xe_hi, 6, half)
                i.then_inc(S["xe_lo_ready"], 1)

            def act_rest(n):
                for half in range(2):
                    dve.wait_ge(S["at_ready"], 2 * n + (half + 1))
                    rest(act_lo, act_hi, 0, half).then_inc(S["at_lo_ready"], 1)

            def slot_gates(n):
                dve.wait_ge(S["kept_used"], n + 2)
                dve.reduce_sum(gate_of[:, 0:1], bank[7][:, 0:3], AX.X).then_inc(S["gate_ready"], 1)

            def out_lo(n):
                dve.wait_ge(S["ye_ready"], n + 1)
                for half in range(2):
                    i = dve.scalar_tensor_tensor(ye_lo[:, hb(0, half)], bank[4 + half][:, :], gate_of[:, 0:1],
                                                 ye_hi[:, hb(0, half)].bitcast(F32), ALU.mult, ALU.subtract)
                i.then_inc(S["ye_lo_ready"], 1)

            def swiglu(n):
                for q in range(4):
                    v = bank[q][:, :].rearrange("p (f two) -> p f two", two=2)
                    dve.wait_ge(S["gu_psum"], n * 4 + (q + 1))
                    dve.tensor_scalar(glu[:, q, :], v[:, :, 0], LIMIT, None, ALU.min).then_inc(S["glu_ready"], 1)
                    dve.tensor_scalar(lin[:, q, :], v[:, :, 1], -LIMIT, LIMIT, ALU.max, ALU.min
                                      ).then_inc(S["lin_ready"], 1)
                for half in range(2):
                    for q in (2 * half, 2 * half + 1):
                        dve.wait_ge(S["lin_ready"], n * 4 + (q + 1))
                        dve.scalar_tensor_tensor(lin[:, q, :], lin[:, q, :], 1.0, glu[:, q, :], ALU.add, ALU.mult
                                                 ).then_inc(S["prod_ready"], 1)
                    for q in (2 * half, 2 * half + 1):
                        dve.wait_ge(S["prod_ready"], n * 4 + (q + 1))
                        dve.wait_ge(S["sig_ready"], n * 4 + (q + 1))
                        dve.tensor_tensor(lin[:, q, :], lin[:, q, :], sig[:, q, :], ALU.mult
                                          ).then_inc(S["act_ready"], 1)

            def add_up(n, pieces=range(6)):
                for i in pieces:
                    c, half = i // 2, i % 2
                    dve.wait_ge(S["cm_psum"], n * 6 + (i + 1))
                    dve.tensor_tensor(hid[0:rows(c), c, hb(c, half)], hid[0:rows(c), c, hb(c, half)],
                                      bank[2 + i % 2][0:rows(c), :], ALU.add).then_inc(S["cm_done"], 1)

            select(0, 0, 0)
            wlink = chain(dve, work_chain)
            dve.wait_ge(S["cnt_psum"], 1)
            for i in range(2):
                wlink(dve.tensor_scalar(flags[0:1, i, :], bank[2][0:1, 0:E], float(P * (i + 1)), None, ALU.is_gt))
            f = flags[0:1].rearrange("p a b -> p (a b)")
            wlink(dve.tensor_tensor_scan(ranks[0:1], ones[0:1, 0:2 * E], f, 0.0, ALU.mult, ALU.add))
            wlink(dve.tensor_tensor(match[0:1], ranks[0:1].unsqueeze(1).to_broadcast([1, MAX_EXTRA, 2 * E]),
                                    slots[0:1, 1:1 + MAX_EXTRA].unsqueeze(2).to_broadcast([1, MAX_EXTRA, 2 * E]),
                                    ALU.is_equal))
            wlink(dve.tensor_tensor(match[0:1], match[0:1], f.unsqueeze(1).to_broadcast([1, MAX_EXTRA, 2 * E]),
                                    ALU.mult))
            wlink(dve.tensor_tensor(match[0:1], match[0:1],
                                    slots[0:1, 0:2 * E].unsqueeze(1).to_broadcast([1, MAX_EXTRA, 2 * E]), ALU.mult))
            wlink(dve.reduce_sum(codes[0:1, 0:MAX_EXTRA], match[0:1], AX.X))
            wlink(dve.tensor_copy(work[0:1, 48:48 + MAX_EXTRA], codes[0:1, 0:MAX_EXTRA]))
            wlink(dve.tensor_copy(work[0:1, 32:33], ranks[0:1, 2 * E - 1:2 * E]))
            wlink(dve.tensor_scalar(work[0:1, 0:MAX_EXTRA], work[0:1, 48:48 + MAX_EXTRA], E - 1, None,
                                    ALU.bitwise_and))
            wlink(dve.tensor_scalar(work[0:1, 16:16 + MAX_EXTRA], work[0:1, 48:48 + MAX_EXTRA], 5, 7,
                                    ALU.logical_shift_right, ALU.logical_shift_left))
            dve.sem_inc(S["work_ready"], 1)
            for n in range(6):
                c, half = n // 2, n % 2
                dve.wait_ge(S["bd_psum"], n + 1)
                dve.tensor_tensor(hid[0:rows(c), c, hb(c, half)], hid[0:rows(c), c, hb(c, half)],
                                  bank[4 + n % 2][0:rows(c), :], ALU.add).then_inc(S["bd_done"], 1)

            link(dve.tensor_copy(gates3[:, :, :, 0], gates))
            link(dve.tensor_tensor(gates_rest, gates, gates3[:, :, :, 0], ALU.subtract))
            link(dve.tensor_copy(gates3[:, :, :, 1], gates_rest))
            link(dve.tensor_tensor(gates3[:, :, :, 2], gates_rest, gates3[:, :, :, 1], ALU.subtract))
            dve.wait_ge(S["bd_done"], 6)
            dve.sem_inc(S["early_done"], 1)

            def block_of(n, first=False, last=False):
                pick(n, n)
                for j in range(LEAD, 6):
                    split_lo(n, j)
                if not last:
                    select(n + 1, n + 1, 0)
                for j in range(6, 7 + LEAD):
                    split_lo(n, j)
                swiglu(n)
                split_lo(n, 7 + LEAD)
                act_rest(n)
                if not first:
                    add_up(n - 1, (0, 1))
                if not last:
                    inputs_lo(n + 1)
                if not first:
                    add_up(n - 1, (2, 3))
                for j in range(8 + LEAD, EXPERT_CHUNKS):
                    split_lo(n, j)
                if not first:
                    add_up(n - 1, (4, 5))
                slot_gates(n)
                if not last:
                    for j in range(LEAD):
                        split_lo(n + 1, j)
                out_lo(n)

            for j in range(LEAD):
                split_lo(0, j)
            inputs_lo(0)
            block_of(0, first=True)
            with dve.Fori(1, E - 1) as n:
                block_of(n)
            block_of(E - 1, last=True)
            add_up(E - 1)
            dve.wait_ge(S["cm_done"], 6 * E)
            more = dve.value_load(work[0:1, 32:33], min_val=0, max_val=MAX_EXTRA)
            with dve.If(more > 0):
                with dve.Fori(0, more) as i:
                    n = i + E
                    e = dve.value_load(work[0:1, bass.ds(i, 1)], min_val=0, max_val=E - 1)
                    b = dve.value_load(work[0:1, bass.ds(i + 16, 1)], min_val=0, max_val=P)
                    pick(n, e)
                    select(n, e, b + P)
                    for j in range(LEAD):
                        split_lo(n, j)
                    inputs_lo(n)
                    for j in range(LEAD, 7 + LEAD):
                        split_lo(n, j)
                    swiglu(n)
                    split_lo(n, 7 + LEAD)
                    act_rest(n)
                    for j in range(8 + LEAD, EXPERT_CHUNKS):
                        split_lo(n, j)
                    slot_gates(n)
                    out_lo(n)
                    add_up(n)
                    dve.wait_ge(S["cm_done"], n * 6 + 6)
            dve.sem_inc(S["all_added"], 1)
            for c in range(3):
                dve.wait_ge(S["y_ss"], c + 1)
                var(small[0:rows(c), 28 + c:29 + c], c, D).then_inc(S["y_var"], 1)
            for c in range(3):
                dve.wait_ge(S["y_std"], c + 1)
                link(dve.reciprocal(small[0:rows(c), 12 + c:13 + c], small[0:rows(c), 32 + c:33 + c]))
                dve.scalar_tensor_tensor(hid[0:rows(c), c, :], hid[0:rows(c), c, :], small[0:rows(c), 12 + c:13 + c],
                                         nl_row[0:rows(c)], ALU.mult, ALU.mult).then_inc(S["y_out"], 1)


_INS = ["x_prompt", "x_sample", "state_conv", "state_ssm", "norm_mix", "w_in", "conv_w", "conv_b", "dt_bias",
        "a_log", "d_skip", "gnorm_w", "v_norm_w", "v_norm_b", "w_spatial", "b_spatial", "w_branch_ssd",
        "w_branch_mlp", "w_out", "norm_ffn", "w_router", "b_router", "w_gu", "b_gu", "w_down", "b_down",
        "norm_final"]
_OUTS = [(1, SEQ, D), (DB, DS, D), (1, 1, KEEP, CONV), (1, 1, H, HP, N), (1, DB, KEEP, CONV),
         (1, DB, H, HP, N), (1, DB, DS, D)]


def kernel(**inputs):
    import numpy as np
    import concourse.bacc as bacc
    from concourse.bass_utils import run_bass_kernel_spmd

    nc = bacc.Bacc("TRN2", target_bir_lowering=False, num_devices=1)
    arrays, args = {}, []
    for name in _INS:
        a = np.ascontiguousarray(inputs[name])
        arrays[f"in_{name}"] = a
        args.append(nc.dram_tensor(f"in_{name}", a.shape, mybir.dt.from_np(a.dtype), kind="ExternalInput").ap())
    for i, shape in enumerate(_OUTS):
        args.append(nc.dram_tensor(f"out_{i}", shape, F32, kind="ExternalOutput").ap())
    build(nc, *args)
    r = run_bass_kernel_spmd(nc, [arrays], core_ids=[0])
    return tuple(r.results[0][f"out_{i}"] for i in range(len(_OUTS)))
```
